# Optimizing a Trainium2 kernel written in Bass

```python
import jax, jax.numpy as jnp
from jax import lax
import numpy as np

D_MODEL = 1024
BATCH = 1
SEQ = 512
DEPTH = 2

CHUNK = 64
HEAD_DIM = 64
A_Q_HEADS = 8
A_KV_HEADS = 2
A_WINDOW_CHUNKS = 1
B_CHANNELS = 512
B_CONV = 3
C_HEADS = 8
C_BACK_CHUNKS = 8
C_REL_MAX = 256
C_REL_SIZE = CHUNK + C_REL_MAX
D_FF = 2816
FFN_CONV = 3
ROPE_THETA = 10000.0
EPS = 1e-6
NEG_INF = -1e30
N_BRANCHES = 3

A_Q = A_Q_HEADS * HEAD_DIM
A_KV = A_KV_HEADS * HEAD_DIM
C_W = C_HEADS * HEAD_DIM
SPLIT_SIZES = (A_Q, A_KV, A_KV, B_CHANNELS, B_CHANNELS, B_CHANNELS, C_W, C_W, C_W, N_BRANCHES * D_MODEL)
IN_COLS = A_Q + 2 * A_KV + 3 * B_CHANNELS + 3 * C_W + N_BRANCHES * D_MODEL

kernel_name = "chunk_causal_hybrid_gated_trunk"

def rmsnorm(x, g):
    xf = x.astype(jnp.float32)
    y = xf * lax.rsqrt(jnp.mean(xf * xf, axis=-1, keepdims=True) + EPS)
    return (y * g.astype(jnp.float32)).astype(x.dtype)

def rope(t, pos):
    half = HEAD_DIM // 2
    inv = ROPE_THETA ** (-jnp.arange(half, dtype=jnp.float32) / half)
    ang = pos.astype(jnp.float32)[:, None] * inv[None, :]
    cos = jnp.cos(ang)[None, :, None, :]
    sin = jnp.sin(ang)[None, :, None, :]
    tf = t.astype(jnp.float32)
    t1, t2 = tf[..., :half], tf[..., half:]
    out = jnp.concatenate([t1 * cos - t2 * sin, t2 * cos + t1 * sin], axis=-1)
    return out.astype(t.dtype)

def causal_dwconv(x, w):
    k_w = w.shape[0]
    s = x.shape[1]
    xp = jnp.pad(x, ((0, 0), (k_w - 1, 0), (0, 0)))
    out = xp[:, 0:s] * w[0]
    for k in range(1, k_w):
        out = out + xp[:, k:k + s] * w[k]
    return out

def chunk_band(t, n_back):
    b, s = t.shape[0], t.shape[1]
    nc = s // CHUNK
    tc = t.reshape((b, nc, CHUNK) + t.shape[2:])
    tp = jnp.pad(tc, [(0, 0), (n_back, 0)] + [(0, 0)] * (tc.ndim - 2))
    band = jnp.stack([tp[:, j:j + nc] for j in range(n_back + 1)], axis=2)
    return band.reshape((b, nc, (n_back + 1) * CHUNK) + t.shape[2:])

def band_valid(nc, n_back):
    ci = jnp.arange(nc)[:, None] - n_back + jnp.arange(n_back + 1)[None, :]
    return jnp.repeat(ci >= 0, CHUNK, axis=1)

def window_gqa_sinks(q, k, v, sinks):
    b, s = q.shape[0], q.shape[1]
    nc = s // CHUNK
    grp = A_Q_HEADS // A_KV_HEADS
    qc = q.reshape(b, nc, CHUNK, A_KV_HEADS, grp, HEAD_DIM)
    kb = chunk_band(k, A_WINDOW_CHUNKS)
    vb = chunk_band(v, A_WINDOW_CHUNKS)
    scores = jnp.einsum('bcqkgd,bcskd->bckgqs', qc, kb).astype(jnp.float32) * (HEAD_DIM ** -0.5)
    valid = band_valid(nc, A_WINDOW_CHUNKS)[None, :, None, None, None, :]
    scores = jnp.where(valid, scores, NEG_INF)
    sink = jnp.broadcast_to(sinks.astype(jnp.float32).reshape(1, 1, A_KV_HEADS, grp, 1, 1),
                            scores.shape[:-1] + (1,))
    p = jax.nn.softmax(jnp.concatenate([scores, sink], axis=-1), axis=-1)[..., :-1]
    out = jnp.einsum('bckgqs,bcskd->bcqkgd', p.astype(v.dtype), vb)
    return out.reshape(b, s, A_Q)

def chunk_relbias_attention(q, k, v, rel_table):
    b, s = q.shape[0], q.shape[1]
    nc = s // CHUNK
    band = (C_BACK_CHUNKS + 1) * CHUNK
    qc = q.reshape(b, nc, CHUNK, C_HEADS, HEAD_DIM)
    kb = chunk_band(k, C_BACK_CHUNKS)
    vb = chunk_band(v, C_BACK_CHUNKS)
    scores = jnp.einsum('bcqhd,bcshd->bchqs', qc, kb).astype(jnp.float32) * (HEAD_DIM ** -0.5)
    q_local = jnp.arange(CHUNK)
    k_off = jnp.arange(band) - C_BACK_CHUNKS * CHUNK
    rel = jnp.clip(q_local[:, None] - k_off[None, :], -(CHUNK - 1), C_REL_MAX) + (CHUNK - 1)
    bias = rel_table.astype(jnp.float32)[:, rel]
    valid = band_valid(nc, C_BACK_CHUNKS)[None, :, None, None, :]
    scores = jnp.where(valid, scores + bias[None, None], NEG_INF)
    p = jax.nn.softmax(scores, axis=-1)
    out = jnp.einsum('bchqs,bcshd->bcqhd', p.astype(v.dtype), vb)
    return out.reshape(b, s, C_W)

def setup_inputs(seed: int = 0) -> dict:
    key = jax.random.key(seed)
    ks = jax.random.split(key, 16)
    f32 = jnp.float32

    def nrm(k, shape, scale):
        return jax.random.normal(k, shape, f32) * scale

    return {
        "x": nrm(ks[0], (BATCH, SEQ, D_MODEL), 1.0),
        "mix_norm_g": 1.0 + nrm(ks[1], (DEPTH, D_MODEL), 0.05),
        "w_in": nrm(ks[2], (DEPTH, D_MODEL, IN_COLS), D_MODEL ** -0.5),
        "attn_sinks": nrm(ks[3], (DEPTH, A_Q_HEADS), 1.0),
        "conv_b_w": nrm(ks[4], (DEPTH, B_CONV, B_CHANNELS), B_CONV ** -0.5),
        "rel_bias": nrm(ks[5], (DEPTH, C_HEADS, C_REL_SIZE), 0.2),
        "w_o_a": nrm(ks[6], (DEPTH, A_Q, D_MODEL), A_Q ** -0.5),
        "w_o_b": nrm(ks[7], (DEPTH, B_CHANNELS, D_MODEL), B_CHANNELS ** -0.5),
        "w_o_c": nrm(ks[8], (DEPTH, C_W, D_MODEL), C_W ** -0.5),
        "w_out": nrm(ks[9], (DEPTH, D_MODEL, D_MODEL), D_MODEL ** -0.5),
        "ffn_norm_g": 1.0 + nrm(ks[10], (DEPTH, D_MODEL), 0.05),
        "w_up": nrm(ks[11], (DEPTH, D_MODEL, 2 * D_FF), D_MODEL ** -0.5),
        "ffn_conv_w": nrm(ks[12], (DEPTH, FFN_CONV, 2 * D_FF), FFN_CONV ** -0.5),
        "w_down": nrm(ks[13], (DEPTH, D_FF, D_MODEL), D_FF ** -0.5),
        "final_norm_g": 1.0 + nrm(ks[14], (D_MODEL,), 0.05),
    }

def reference(x, mix_norm_g, w_in, attn_sinks, conv_b_w, rel_bias, w_o_a, w_o_b, w_o_c,
              w_out, ffn_norm_g, w_up, ffn_conv_w, w_down, final_norm_g):
    b, s, d = x.shape
    pos = jnp.arange(s, dtype=jnp.int32)
    split_idx = np.cumsum(SPLIT_SIZES)[:-1].tolist()
    for l in range(DEPTH):
        h = rmsnorm(x, mix_norm_g[l])
        proj = h @ w_in[l]
        qa, ka, va, bg, cg, ub, qc, kc, vc, gl = jnp.split(proj, split_idx, axis=-1)

        qa = rope(qa.reshape(b, s, A_Q_HEADS, HEAD_DIM), pos)
        ka = rope(ka.reshape(b, s, A_KV_HEADS, HEAD_DIM), pos)
        va = va.reshape(b, s, A_KV_HEADS, HEAD_DIM)
        ya = window_gqa_sinks(qa, ka, va, attn_sinks[l]) @ w_o_a[l]

        yb = (bg * causal_dwconv(cg * ub, conv_b_w[l])) @ w_o_b[l]

        qc = qc.reshape(b, s, C_HEADS, HEAD_DIM)
        kc = kc.reshape(b, s, C_HEADS, HEAD_DIM)
        vc = vc.reshape(b, s, C_HEADS, HEAD_DIM)
        yc = chunk_relbias_attention(qc, kc, vc, rel_bias[l]) @ w_o_c[l]

        gates = jax.nn.sigmoid(gl.astype(jnp.float32)).astype(x.dtype).reshape(b, s, N_BRANCHES, d)
        mixed = gates[:, :, 0] * ya + gates[:, :, 1] * yb + gates[:, :, 2] * yc
        x = x + mixed @ w_out[l]

        h = rmsnorm(x, ffn_norm_g[l])
        up = causal_dwconv(h @ w_up[l], ffn_conv_w[l])
        gate, val = jnp.split(up, 2, axis=-1)
        x = x + (jax.nn.silu(gate) * val) @ w_down[l]
    return rmsnorm(x, final_norm_g)


_drawn_inputs = setup_inputs


def setup_inputs(seed=0):
    import zlib

    import numpy as np

    out = dict(_drawn_inputs(seed))
    spreads = {}
    factors = {'attn_sinks': 8.0, 'rel_bias': 3.185}
    for name, (base, spread) in spreads.items():
        noise = np.random.default_rng([zlib.crc32(name.encode()), seed]).standard_normal(out[name].shape)
        drawn = base * np.exp(spread * noise) if base else spread * noise
        out[name] = __import__('jax').numpy.asarray(drawn.astype(out[name].dtype))
    for name, factor in factors.items():
        out[name] = (out[name] * factor).astype(out[name].dtype)
    return out
```

```python
from contextlib import ExitStack

import numpy as np

import concourse.bass as bass
from concourse import mybir

F32 = mybir.dt.float32
F32R = mybir.dt.float32r
ALU = mybir.AluOpType
ACT = mybir.ActivationFunctionType

P = 128
D_MODEL = 1024
SEQ = 512
DEPTH = 2
CHUNK = 64
HEAD_DIM = 64
A_Q_HEADS = 8
A_KV_HEADS = 2
B_CHANNELS = 512
C_HEADS = 8
C_REL_MAX = 256
C_REL_SIZE = CHUNK + C_REL_MAX
D_FF = 2816
TAPS = 3
ROPE_THETA = 10000.0
EPS = 1e-6
MASKED = -1e30
NO_MAX_YET = 3e38

KT = D_MODEL // P
TT = SEQ // P
HALF = P // 2
PAIRS = 4
FF_T = D_FF // P
SCALE = HEAD_DIM ** -0.5

TILES = 8
U_A = 0
U_C = U_A + 6
U_B = U_C + 12
U_MERGE = U_B + 12
U_OUT = U_MERGE + 36
U_UP = U_OUT + KT
U_DOWN = U_UP + 2 * FF_T
UNITS = U_DOWN + FF_T * KT // TILES
assert UNITS % 4 == 0 and U_UP % 2 == 0 and (U_UP + 4) % 4 == (U_UP % 4)
RAW_SLOTS, HI_SLOTS, LO_SLOTS = 4, 4, 2

PROJ_BANKS = 3
SCORE_BANK, PT_BANK, O_BANK = 3, 5, 7
MS_BANK, RB_BANK = 5, 6

O_OUT = U_MERGE + 3 * 2 * KT
O_UP = O_OUT + KT
O_DOWN = O_UP + 2 * FF_T
OUTS = O_DOWN + KT

A_START = U_C + 1
C_START = U_MERGE + 14

PG2, PGN, PCB, PCF = 0, KT, 2 * KT, 2 * KT + 4 * TAPS
PSK = PCF + 2 * FF_T * TAPS
NPAR = PSK + A_Q_HEADS

REL_EXT = 2 * SEQ


class Tally:

    def __init__(self, sem, per_layer, credit=0):
        self.sem, self.per_layer, self.credit = sem, per_layer, credit

    def after(self, l, n):
        return l * self.per_layer + (n + (1 + self.credit))


def merge_group(u):
    g, part = divmod(u - U_MERGE, 3)
    return g // 4, g % 4, part


def unit_outs(u):
    if u < U_MERGE:
        return [u]
    g, part = divmod(u - U_MERGE, 3)
    first = U_MERGE + 4 * g
    return [[first], [first + 1], [first + 2, first + 3]][part]


def head_at(slot):
    for off, start in ((0, A_START), (8, C_START)):
        h = slot - start
        if 0 <= h < 8 + 2:
            return off, (h if h < 8 else None), (h - 1 if 0 <= h - 1 < 8 else None), (h - 2 if 0 <= h - 2 < 8 else None)
    return None


def item(off, h, t):
    return (off + h) * TT + t


def key_tiles(off, t):
    return list(range(max(t - 1, 0), t + 1)) if off == 0 else list(range(t + 1))


def build_trunk(nc, xT, weights, g_first, params, rope, rel, outT):
    ctx = ExitStack()
    with ctx:
        def sb(name, shape, dt=F32):
            return ctx.enter_context(nc.sbuf_tensor(name, shape, dt))

        def sem(name):
            return ctx.enter_context(nc.semaphore(name))

        rel_ext_dram = nc.dram_tensor("rel_ext_dram", [DEPTH * C_HEADS, REL_EXT], F32, kind="Internal").ap()

        x = sb("x", [P, KT, SEQ])
        xg_hi = sb("xg_hi", [P, KT, SEQ], F32R)
        xg_lo = sb("xg_lo", [P, KT, SEQ], F32R)
        rnorm = sb("rnorm", [P, SEQ])
        sq_sum = sb("sq_sum", [P, SEQ])
        raw = sb("raw", [P, RAW_SLOTS, TILES * P])
        w_hi = sb("w_hi", [P, HI_SLOTS, TILES * P], F32R)
        w_lo = sb("w_lo", [P, LO_SLOTS, TILES * P], F32R)
        par_all = sb("par_all", [P, DEPTH, NPAR])
        par = sb("par", [P, NPAR])
        g0 = sb("g0", [P, KT])
        neg_sink = sb("neg_sink", [P, A_Q_HEADS])
        ident = sb("ident", [P, P])
        ones = sb("ones", [P, 1])
        minus_half = sb("minus_half", [P, TT])
        ms = sb("ms", [P, TT])
        r_tok = sb("r_tok", [P, TT])
        mask_a = sb("mask_a", [P, 2 * P])
        neg_max = sb("neg_max", [P, 16 * TT])
        denom = sb("denom", [P, 16 * TT])
        sink_e = sb("sink_e", [P, 8 * TT])
        tmp = [sb(f"tmp{i}", [P, SEQ + 2]) for i in range(4)]

        sb("zone", [P, 44 * SEQ])
        zone_at = nc.sbuf_base - 4 * 44 * SEQ
        sb("soft", [P, 1280 + TT * SEQ])
        soft_at = nc.sbuf_base - 4 * (1280 + TT * SEQ)

        def view(name, base, start, shape, dt=F32):
            return nc.alloc_sbuf_tensor_at(name, [P] + shape, dt, offset=base + 4 * start)

        T = SEQ
        qa = view("qa", zone_at, 0, [PAIRS, T])
        ka = view("ka", zone_at, 4 * T, [T])
        va = view("va", zone_at, 5 * T, [TT, P])
        rope_sb = view("rope_sb", zone_at, 6 * T, [2, T])
        merged = view("merged", zone_at, 0, [KT, T])
        qc = view("qc", zone_at, 8 * T, [PAIRS, T])
        kc = view("kc", zone_at, 12 * T, [PAIRS, T])
        vc = view("vc", zone_at, 16 * T, [TT, T])
        bias = view("bias", zone_at, 20 * T, [C_HEADS, T])
        mix_hi = view("mix_hi", zone_at, 8 * T, [KT, T], F32R)
        mix_lo = view("mix_lo", zone_at, 16 * T, [KT, T], F32R)
        ya_hi = view("ya_hi", zone_at, 28 * T, [PAIRS, T], F32R)
        ya_lo = view("ya_lo", zone_at, 32 * T, [PAIRS, T], F32R)
        ybc_hi = view("ybc_hi", zone_at, 36 * T, [PAIRS, T], F32R)
        ybc_lo = view("ybc_lo", zone_at, 40 * T, [PAIRS, T], F32R)
        ff_hi = view("ff_hi", zone_at, 0, [FF_T, T], F32R)
        ff_lo = view("ff_lo", zone_at, FF_T * T, [FF_T, T], F32R)
        prob = [view(f"prob{t}", soft_at, 64 * t * (t + 1), [(t + 1) * P]) for t in range(TT)]
        prob_t = view("prob_t", soft_at, 1280, [TT, T])
        wide = [view(f"wide{i}", soft_at, T * i, [T]) for i in range(6)]
        x_out = view("x_out", zone_at, 0, [KT, T])
        rel_tab = view("rel_tab", soft_at, 0, [C_REL_SIZE])
        rel_ext = view("rel_ext", soft_at, T, [REL_EXT])

        psum = ctx.enter_context(nc.psum_tensor("psum", [P, 8, SEQ], F32))

        raw_in = [sem(f"raw_in{i}") for i in range(RAW_SLOTS)]
        x_in = [sem(f"x_in{i}") for i in range(4)]
        g_in, par_in, rope_in, rel_in, bias_in = (sem(n) for n in ("g_in", "par_in", "rope_in", "rel_in", "bias_in"))
        rel_built, rel_stored, out_stored = sem("rel_built"), sem("rel_stored"), sem("out_stored")
        ident_set, consts_set, bias_masked, scores_seen = sem("ident_set"), sem("consts_set"), sem("bias_masked"), sem("scores_seen")
        zeros_set = sem("zeros_set")
        unit_steps = Tally(sem("unit_steps"), 2 * UNITS, 2 * HI_SLOTS)
        scores_done = Tally(sem("scores_done"), 16 * TT)
        probt_done = Tally(sem("probt_done"), 16 * TT)
        vt_done = Tally(sem("vt_done"), 5)
        pv_done = Tally(sem("pv_done"), 16)
        sumsq_done = Tally(sem("sumsq_done"), 2)
        rb_done = Tally(sem("rb_done"), 2)
        hi_ready = Tally(sem("hi_ready"), UNITS - 1, -1)
        xhi_ready = Tally(sem("xhi_ready"), 2 * KT)
        sq_ready = Tally(sem("sq_ready"), 2 * KT, -KT)
        rnorm_ready = Tally(sem("rnorm_ready"), 2)
        rot_done = Tally(sem("rot_done"), 5)
        v_ready = Tally(sem("v_ready"), 5)
        tapb_done = Tally(sem("tapb_done"), 4)
        yb_hi_ready = Tally(sem("yb_hi_ready"), 4)
        exp_done = Tally(sem("exp_done"), 16 * TT)
        sink_done = Tally(sem("sink_done"), 8 * TT)
        probt_ready = Tally(sem("probt_ready"), 16 * TT)
        o_hi_ready = Tally(sem("o_hi_ready"), 8)
        gate_ready = Tally(sem("gate_ready"), 3 * KT)
        mix_hi_ready = Tally(sem("mix_hi_ready"), KT)
        ff_act = Tally(sem("ff_act"), 4 * FF_T)
        evac = Tally(sem("evac"), OUTS, 4)
        xlo_ready = Tally(sem("xlo_ready"), 2 * KT)
        sum_step = Tally(sem("sum_step"), 2 * (KT - 1))
        ms_ready = Tally(sem("ms_ready"), 2)
        par_ready = Tally(sem("par_ready"), 1)
        nsink_ready = Tally(sem("nsink_ready"), 1)
        rope_mul = Tally(sem("rope_mul"), 10)
        qk_ready = Tally(sem("qk_ready"), 5)
        convb = Tally(sem("convb"), 20)
        logits_ready = Tally(sem("logits_ready"), 16 * TT)
        denom_done = Tally(sem("denom_done"), 8 * TT)
        recip_done = Tally(sem("recip_done"), 16 * TT)
        prob_ready = Tally(sem("prob_ready"), 16 * TT)
        o_lo_ready = Tally(sem("o_lo_ready"), 8)
        merged_sum = Tally(sem("merged_sum"), 2 * KT)
        mix_lo_ready = Tally(sem("mix_lo_ready"), KT)
        ff_vec = Tally(sem("ff_vec"), 7 * FF_T)
        out_ready = sem("out_ready")
        first_squares = sem("first_squares")
        hi0_ready = Tally(sem("hi0_ready"), 1)
        lo_ready = Tally(sem("lo_ready"), UNITS, RAW_SLOTS)
        rtok_ready = Tally(sem("rtok_ready"), 2)

        def hi_used(l, u):
            return unit_steps.after(l, 2 * u)

        def unit_done(l, u):
            return unit_steps.after(l, 2 * u + 1)

        def wait(eng, tally, l, n):
            eng.wait_ge(tally.sem, tally.after(l, n))

        def hi_wait(eng, l, u):
            if isinstance(u, int) and u == 0:
                wait(eng, hi0_ready, l, 0)
            else:
                wait(eng, hi_ready, l, u)

        block = ctx.enter_context(nc.Block())

        @block.sync
        def _(sp):
            def load_units(l, quad):
                for slot in range(RAW_SLOTS):
                    u = quad * RAW_SLOTS + slot
                    sp.wait_ge(lo_ready.sem, lo_ready.after(l, u - RAW_SLOTS))
                    sp.dma_start(raw[:, slot, :],
                                 weights[bass.ds(l * UNITS + u, 1)].rearrange("a p n -> p (a n)")
                                 ).then_inc(raw_in[slot], 16)

            def load_rope(l):
                sp.wait_ge(unit_steps.sem, unit_steps.after(l, -1))
                sp.dma_start(rope_sb[:], rope).then_inc(rope_in, 16)

            def load_bias(l):
                sp.wait_ge(rel_stored, 16)
                rows = bass.AP(tensor=rel_ext_dram.tensor, offset=0,
                               ap=[[C_HEADS * REL_EXT, DEPTH], [1, P], [REL_EXT, C_HEADS], [1, SEQ]])
                sp.dma_start(bias[:], rows[bass.ds(l, 1)].rearrange("a p h n -> (a p) h n")).then_inc(bias_in, 16)

            for i in range(4):
                sp.dma_start(x[:, 2 * i:2 * i + 2, :], xT.rearrange("(k p) t -> p k t", p=P)[:, 2 * i:2 * i + 2, :]
                             ).then_inc(x_in[i], 16)
            with sp.Fori(0, DEPTH) as l:
                load_units(l, 0)
                load_rope(l)
                with sp.Fori(1, U_B // RAW_SLOTS + 1) as q:
                    load_units(l, q)
                load_bias(l)
                with sp.Fori(U_B // RAW_SLOTS + 1, UNITS // RAW_SLOTS) as q:
                    load_units(l, q)
            for k in range(KT):
                sp.wait_ge(out_ready, k + 1)
                sp.dma_start(outT.rearrange("(k p) t -> p k t", p=P)[:, k, :],
                             x_out[:, k, :]).then_inc(out_stored, 16)
            sp.wait_ge(out_stored, 16 * KT)

        @block.gpsimd
        def _(pool):
            pool.sem_inc(lo_ready.sem, lo_ready.credit)
            nc.gpsimd.memset(ident[:], 0.0).then_inc(zeros_set, 1)
            pool.wait_ge(zeros_set, 1)
            nc.gpsimd.affine_select(out=ident[:], in_=ident[:], compare_op=ALU.not_equal, fill=1.0, base=0,
                                    pattern=[[-1, P]], channel_multiplier=1).then_inc(ident_set, 1)

            def lo_part(l, u, raw_slot, lo_slot):
                hi_wait(pool, l, u)
                pool.wait_ge(unit_steps.sem, unit_done(l, u - LO_SLOTS))
                nc.gpsimd.tensor_tensor(w_lo[:, lo_slot, :], raw[:, raw_slot, :],
                                        w_hi[:, raw_slot, :].bitcast(F32), ALU.subtract).then_inc(lo_ready.sem, 1)

            def first_hi_part(l):
                pool.wait_ge(unit_steps.sem, hi_used(l, -HI_SLOTS))
                pool.wait_ge(raw_in[0], l * (16 * (UNITS // RAW_SLOTS)) + 16)
                nc.gpsimd.tensor_tensor(w_hi[:, 0, :], raw[:, 0, :],
                                        ones[:, 0:1].to_broadcast([P, TILES * P]), ALU.mult).then_inc(hi0_ready.sem, 1)

            def row_factors(l, norm):
                wait(pool, ms_ready, l, norm)
                nc.gpsimd.tensor_tensor(r_tok[:], ms[:], minus_half[:], ALU.pow).then_inc(rtok_ready.sem, 1)

            pool.wait_ge(consts_set, 1)
            with pool.Fori(0, DEPTH) as l:
                first_hi_part(l)
                lo_part(l, 0, 0, 0)
                lo_part(l, 1, 1, 1)
                row_factors(l, 0)
                with pool.Fori(0, (U_UP - 2) // 4) as q:
                    for j in range(2, 6):
                        lo_part(l, q * 4 + j, j % 4, j % 2)
                lo_part(l, U_UP, U_UP % 4, 0)
                lo_part(l, U_UP + 1, (U_UP + 1) % 4, 1)
                row_factors(l, 1)
                with pool.Fori((U_UP + 2) // 4, UNITS // 4) as q:
                    for j in range(4):
                        lo_part(l, q * 4 + j, j, j % 2)
            row_factors(DEPTH, 0)

        @block.scalar
        def _(act):
            def hi_part(l, u, slot):
                act.wait_ge(unit_steps.sem, hi_used(l, u - HI_SLOTS))
                act.wait_ge(raw_in[slot], l * (16 * (UNITS // 4)) + (u - slot) * 4 + 16)
                nc.scalar.copy(w_hi[:, slot, :], raw[:, slot, :]).then_inc(hi_ready.sem, 1)

            def split_x(l, norm, k, gain):
                def hi():
                    nc.scalar.activation(xg_hi[:, k, :], x[:, k, :], ACT.Identity, scale=gain
                                         ).then_inc(xhi_ready.sem, 1)

                def square():
                    nc.scalar.activation(sq_sum[:] if k == 0 else tmp[k % 2][:, 2:], x[:, k, :], ACT.Square
                                         ).then_inc(sq_ready.sem, 1)
                for step in (square, hi) if (norm, k) == (0, KT - 1) else (hi, square):
                    step()

            def row_factor_out(l, norm):
                wait(act, rb_done, l, norm)
                nc.scalar.copy(rnorm[:], psum[:, RB_BANK, :]).then_inc(rnorm_ready.sem, 1)

            def rotate(l, u):
                wait(act, evac, l, u)
                for q in range(4):
                    r = nc.scalar.copy(wide[2 + u % 2][32 * q:32 * q + 32, :],
                                       wide[u % 2][32 * (q ^ 1):32 * (q ^ 1) + 32, :])
                r.then_inc(rot_done.sem, 1)

            def softmax_stage(l, slot):
                stages = head_at(slot)
                if not stages:
                    return
                off, h_s, h_t, h_v = stages
                if h_v is not None and h_v % 2:
                    pair = (off + h_v) // 2
                    hi = ya_hi if off == 0 else ybc_hi
                    wait(act, pv_done, l, off + h_v)
                    nc.scalar.copy(hi[:, h_v // 2, :], psum[:, O_BANK, :]).then_inc(o_hi_ready.sem, 1)
                for t in range(TT):
                    if h_t is not None:
                        n, kts = item(off, h_t, t), key_tiles(off, t)
                        wait(act, probt_done, l, n)
                        nc.scalar.copy(prob_t[:, kts[0]:kts[-1] + 1, t * P:(t + 1) * P],
                                       psum[:, PT_BANK + n % 2, 0:len(kts) * P].rearrange("p (k q) -> p k q", q=P)
                                       ).then_inc(probt_ready.sem, 1)
                    if h_s is not None:
                        n, width = item(off, h_s, t), len(key_tiles(off, t)) * P
                        wait(act, logits_ready, l, n)
                        nc.scalar.activation(prob[t][:, 0:width], prob[t][:, 0:width], ACT.Exp, scale=-1.0,
                                             bias=neg_max[:, n:n + 1], accum_out=denom[:, n:n + 1]
                                             ).then_inc(exp_done.sem, 1)
                        if off == 0:
                            head = h_s // 2 + 4 * (h_s % 2)
                            nc.scalar.activation(sink_e[:, n:n + 1], neg_sink[:, head:head + 1], ACT.Exp, scale=-1.0,
                                                 bias=neg_max[:, n:n + 1]).then_inc(sink_done.sem, 1)

            act.dma_start(g0[:], g_first).then_inc(g_in, 16)
            act.dma_start(rel_tab[0:DEPTH * C_HEADS, :], rel).then_inc(rel_in, 16)
            act.dma_start(par_all[:], params.rearrange("l p n -> p l n")).then_inc(par_in, 16)
            act.wait_ge(g_in, 16)
            for k in range(KT):
                act.wait_ge(x_in[k // 2], 16)
                nc.scalar.activation(xg_hi[:, k, :], x[:, k, :], ACT.Identity, scale=g0[:, k:k + 1]
                                     ).then_inc(xhi_ready.sem, 1)
            act.wait_ge(rel_built, 3)
            act.dma_start(rel_ext_dram, rel_ext[0:DEPTH * C_HEADS, :]).then_inc(rel_stored, 16)
            with act.Fori(0, DEPTH) as l:
                for u in range(1, HI_SLOTS):
                    hi_part(l, u, u)
                for u in range(U_OUT):
                    hi_part(l, u + HI_SLOTS, u % 4)
                    if u == 0:
                        row_factor_out(l, 0)
                    if u < 5:
                        rotate(l, u)
                    if u == U_C + 0 or U_C + 9 <= u < U_C + 13:
                        m = 0 if u == U_C else u - (U_C + 9) + 1
                        wait(act, vt_done, l, m)
                        if m == 0:
                            nc.scalar.copy(va[:], psum[:, PT_BANK, :].rearrange("p (t f) -> p t f", f=P)
                                           ).then_inc(v_ready.sem, 1)
                        else:
                            nc.scalar.copy(vc[:, :, (m - 1) * P:m * P],
                                           psum[:, SCORE_BANK + m % 2, :].rearrange("p (t f) -> p t f", f=P)
                                           ).then_inc(v_ready.sem, 1)
                    if U_B <= u < U_MERGE:
                        c, part = divmod(u - U_B, 3)
                        if part == 1:
                            wait(act, convb, l, 5 * c)
                            nc.scalar.activation(wide[2 + c % 2][:], tmp[c % 2][:, 2:], ACT.Identity,
                                                 scale=par[:, PCB + 3 * c + 2:PCB + 3 * c + 3]
                                                 ).then_inc(tapb_done.sem, 1)
                        if part == 2:
                            wait(act, convb, l, 5 * c + 3)
                            nc.scalar.copy(ybc_hi[:, c, :], wide[2 + c % 2][:]).then_inc(yb_hi_ready.sem, 1)
                    if U_MERGE <= u < U_OUT:
                        br, mp, part = merge_group(u)
                        if part < 2:
                            wait(act, evac, l, unit_outs(u)[0])
                            nc.scalar.activation(tmp[2 + part][:, 2:], tmp[part][:, 2:], ACT.Tanh, scale=0.5
                                                 ).then_inc(gate_ready.sem, 1)
                        elif br == 2:
                            for m in (2 * mp, 2 * mp + 1):
                                wait(act, merged_sum, l, KT + m)
                                nc.scalar.activation(mix_hi[:, m, :], merged[:, m, :], ACT.Identity, scale=0.5
                                                     ).then_inc(mix_hi_ready.sem, 1)
                    softmax_stage(l, u + 1)
                for k in range(KT):
                    hi_part(l, U_OUT + HI_SLOTS + k, (U_OUT + k) % 4)
                    wait(act, evac, l, O_OUT + k)
                    split_x(l, 1, k, par[:, PG2 + k:PG2 + k + 1])

                def up_pair(i, b, first=False):
                    for j in range(2):
                        hi_part(l, U_UP + HI_SLOTS + 2 * b + j + i * 4, (U_UP + 2 * b + j) % 4)
                        if first and j == 0:
                            row_factor_out(l, 1)
                        wait(act, evac, l, O_UP + 2 * b + j + i * 4)
                        nc.scalar.activation(wide[2 * b + j][:], tmp[2 * b + j][:, 2:], ACT.Identity,
                                             scale=par[:, bass.ds(i * 6 + (PCF + 3 * (FF_T * j + b) + 2), 1)]
                                             ).then_inc(ff_act.sem, 1)
                    wait(act, ff_vec, l, 7 * b + 2 + i * 14)
                    nc.scalar.activation(wide[4 + b][:], wide[2 * b][:], ACT.Tanh, scale=0.5).then_inc(ff_act.sem, 1)
                    wait(act, ff_vec, l, 7 * b + 5 + i * 14)
                    nc.scalar.copy(ff_hi[:, bass.ds(i * 2 + b, 1), :].rearrange("p a t -> p (a t)"), wide[4 + b][:]
                                   ).then_inc(ff_act.sem, 1)

                up_pair(0, 0, first=True)
                up_pair(0, 1)
                with act.Fori(1, FF_T // 2) as i:
                    up_pair(i, 0)
                    up_pair(i, 1)
                for u in range(U_DOWN, UNITS):
                    if u + HI_SLOTS < UNITS:
                        hi_part(l, u + HI_SLOTS, u % 4)
                    for k in range(KT):
                        if (k * FF_T + FF_T - 1) // TILES == u - U_DOWN:
                            wait(act, evac, l, O_DOWN + k)
                            split_x(l + 1, 0, k, par[:, PGN + k:PGN + k + 1])
            row_factor_out(DEPTH, 0)

        @block.tensor
        def _(pe):
            pe.sem_inc(unit_steps.sem, unit_steps.credit)
            pe.wait_ge(consts_set, 1)
            pe.wait_ge(ident_set, 1)

            def weight_unit(l, u, slot, lo_slot, tiles, before=None, gap=None):
                hi_wait(pe, l, u)
                for i, (dst, a_hi, a_lo, first, _) in enumerate(tiles):
                    if gap and i in (0, 3, 6):
                        gap(i // 3)
                    if before:
                        before(i)
                    w = w_hi[:, slot, i * P:(i + 1) * P]
                    nc.tensor.matmul(dst, w, a_hi, start=first, stop=False)
                    m = nc.tensor.matmul(dst, w, a_lo, start=False, stop=False)
                m.then_inc(unit_steps.sem, 1)
                if gap:
                    gap(3)
                wait(pe, lo_ready, l, u)
                for i, (dst, a_hi, _, _, last) in enumerate(tiles):
                    m = nc.tensor.matmul(dst, w_lo[:, lo_slot, i * P:(i + 1) * P], a_hi, start=False, stop=last)
                m.then_inc(unit_steps.sem, 1)

            def x_tiles(bank):
                return [(psum[:, bank, :], xg_hi[:, k, :], xg_lo[:, k, :], k == 0, k == KT - 1) for k in range(KT)]

            def x_waits(l, norm):
                def before(k):
                    wait(pe, xhi_ready, l, norm * KT + k)
                    wait(pe, xlo_ready, l, norm * KT + k)
                return before

            def sum_squares(l, norm):
                wait(pe, sum_step, l, (norm + 1) * (KT - 1) - 1)
                for t in range(TT):
                    m = nc.tensor.matmul(psum[:, MS_BANK, t:t + 1], sq_sum[:, t * P:(t + 1) * P], ones[:],
                                         start=True, stop=True)
                m.then_inc(sumsq_done.sem, 1)

            def spread_row_factors(l, norm):
                wait(pe, rtok_ready, l, norm)
                for t in range(TT):
                    m = nc.tensor.matmul(psum[:, RB_BANK, t * P:(t + 1) * P],
                                         r_tok[:, t:t + 1].to_broadcast([P, P]), ident[:], start=True, stop=True)
                m.then_inc(rb_done.sem, 1)

            def scores(l, off, h, t):
                n, kts = item(off, h, t), key_tiles(off, t)
                j, at = h // 2, HALF * (h % 2)
                q = (qa if off == 0 else qc)[at:at + HALF, j, t * P:(t + 1) * P]
                keys = slice(kts[0] * P, (kts[-1] + 1) * P)
                k = ka[at:at + HALF, keys] if off == 0 else kc[at:at + HALF, j, keys]
                if h == 0 and t == 0:
                    if off == 0:
                        wait(pe, qk_ready, l, 4)
                    else:
                        wait(pe, v_ready, l, 4)
                if t >= 2 or h > 0:
                    wait(pe, logits_ready, l, n - 2)
                m = nc.tensor.matmul(psum[:, SCORE_BANK + n % 2, 0:len(kts) * P], q, k, start=True, stop=True)
                m.then_inc(scores_done.sem, 1)

            def transpose_probs(l, off, h, t):
                n, kts = item(off, h, t), key_tiles(off, t)
                wait(pe, prob_ready, l, n)
                if n == 0:
                    wait(pe, v_ready, l, 0)
                if t >= 2 or h > 0:
                    wait(pe, probt_ready, l, n - 2)
                for b in range(len(kts)):
                    m = nc.tensor.transpose(psum[:, PT_BANK + n % 2, b * P:(b + 1) * P],
                                            prob[t][:, b * P:(b + 1) * P], ident[:])
                m.then_inc(probt_done.sem, 1)

            def weighted_values(l, off, h):
                at = HALF * (h % 2)
                wait(pe, probt_ready, l, item(off, h, TT - 1))
                if h % 2 == 0 and (off or h):
                    wait(pe, o_lo_ready, l, (off + h) // 2 - 1)
                if off == 0:
                    for t in range(TT):
                        kts = key_tiles(off, t)
                        for kt in kts:
                            m = nc.tensor.matmul(psum[at:at + HALF, O_BANK, t * P:(t + 1) * P],
                                                 va[:, kt, at:at + HALF], prob_t[:, kt, t * P:(t + 1) * P],
                                                 start=(kt == kts[0]), stop=(kt == kts[-1]))
                else:
                    for kt in range(TT):
                        m = nc.tensor.matmul(psum[at:at + HALF, O_BANK, kt * P:],
                                             vc[:, kt, h * HALF:(h + 1) * HALF], prob_t[:, kt, kt * P:],
                                             start=(kt == 0), stop=(kt == TT - 1))
                m.then_inc(pv_done.sem, 1)

            def transpose_values(l, m, u):
                wait(pe, evac, l, u)
                bank = PT_BANK if m == 0 else SCORE_BANK + m % 2
                if m >= 3:
                    wait(pe, v_ready, l, m - 2)
                for t in range(TT):
                    r = nc.tensor.transpose(psum[:, bank, t * P:(t + 1) * P], tmp[u % 2][:, 2 + t * P:2 + (t + 1) * P],
                                            ident[:])
                r.then_inc(vt_done.sem, 1)

            def extra(l, u, gap):
                if (u, gap) == (0, 3):
                    sum_squares(l, 0)
                if (u, gap) == (1, 1):
                    spread_row_factors(l, 0)
                if (u, gap) == (U_C + 1, 0):
                    transpose_values(l, 0, U_C - 1)
                if U_C + 10 <= u < U_C + 14 and gap == 0:
                    transpose_values(l, u - (U_C + 10) + 1, u - 2)
                stages = head_at(u)
                if stages:
                    off, h_s, h_t, h_v = stages
                    if gap == 0 and h_v is not None:
                        weighted_values(l, off, h_v)
                    if h_t is not None:
                        transpose_probs(l, off, h_t, gap)
                    if h_s is not None:
                        scores(l, off, h_s, gap)

            with pe.Fori(0, DEPTH) as l:
                for u in range(U_OUT):
                    outs = unit_outs(u)
                    for o in outs:
                        pe.wait_ge(evac.sem, evac.after(l, o - (PROJ_BANKS if o >= PROJ_BANKS else PROJ_BANKS + 1)))
                    before = x_waits(l, 0) if u == 0 else None
                    if len(outs) == 1:
                        tiles = x_tiles(outs[0] % PROJ_BANKS)
                    else:
                        br, mp, _ = merge_group(u)
                        y_hi, y_lo = (ya_hi, ya_lo) if br == 1 else (ybc_hi, ybc_lo)
                        tiles = [(psum[:, o % PROJ_BANKS, :], y_hi[:, k, :], y_lo[:, k, :], k == 0, k == 3)
                                 for o in outs for k in range(4)]
                        if mp == 0:
                            if br == 0:
                                wait(pe, yb_hi_ready, l, 3)
                                wait(pe, convb, l, 19)
                            else:
                                wait(pe, o_hi_ready, l, 3 if br == 1 else 7)
                                wait(pe, o_lo_ready, l, 3 if br == 1 else 7)
                    weight_unit(l, u, u % 4, u % 2, tiles, before, lambda gap, u=u: extra(l, u, gap))

                with pe.Fori(0, KT // 4) as i:
                    for j in range(4):
                        u = U_OUT + j
                        pe.wait_ge(evac.sem, evac.after(l, O_OUT + j - 3 + i * 4))
                        tiles = [(psum[:, j, :], mix_hi[:, k, :], mix_lo[:, k, :], k == 0, k == KT - 1)
                                 for k in range(KT)]

                        def mix_waits(k):
                            wait(pe, mix_hi_ready, l, k)
                            wait(pe, mix_lo_ready, l, k)
                        weight_unit(l, i * 4 + u, u % 4, u % 2, tiles, mix_waits if j == 0 else None)

                def up_units(i, first=False):
                    for j in range(4):
                        u = U_UP + j

                        def norm_steps(gap, j=j):
                            if (j, gap) == (0, 3):
                                sum_squares(l, 1)
                            if (j, gap) == (1, 1):
                                spread_row_factors(l, 1)
                        pe.wait_ge(evac.sem, evac.after(l, O_UP + j - 4 + i * 4))
                        weight_unit(l, i * 4 + u, u % 4, u % 2, x_tiles(j),
                                    x_waits(l, 1) if first and j == 0 else None, norm_steps if first else None)

                up_units(0, first=True)
                with pe.Fori(1, FF_T // 2) as i:
                    up_units(i)

                for u in range(U_DOWN, UNITS):
                    tiles = []
                    for i in range(TILES):
                        m, k = divmod((u - U_DOWN) * TILES + i, FF_T)
                        if k == 0 or i == 0:
                            wait(pe, evac, l, O_DOWN + m - 4)
                        tiles.append((psum[:, m % 4, :], ff_hi[:, k, :], ff_lo[:, k, :], k == 0, k == FF_T - 1))

                    def ff_waits(i, u=u):
                        pair = (u - U_DOWN) * TILES + i
                        if pair < FF_T:
                            wait(pe, ff_act, l, 4 * pair + 3)
                            wait(pe, ff_vec, l, 7 * pair + 6)
                    weight_unit(l, u, u % 4, u % 2, tiles, ff_waits)
            sum_squares(DEPTH, 0)
            spread_row_factors(DEPTH, 0)

        @block.vector
        def _(dve):
            dve.sem_inc(evac.sem, evac.credit)
            nc.vector.memset(ones[:], 1.0)
            nc.vector.memset(minus_half[:], -0.5)
            for i in range(4):
                nc.vector.memset(tmp[i][:, 0:2], 0.0)
            for half, masked in ((0, (1, 0, 0, 1)), (1, (1, 1, 0, 0))):
                for chunk in range(4):
                    last = nc.vector.memset(mask_a[HALF * half:HALF * half + HALF, chunk * CHUNK:(chunk + 1) * CHUNK],
                                            MASKED if masked[chunk] else 0.0)
            last.then_inc(consts_set, 1)

            def unit_wait(l, u):
                dve.wait_ge(unit_steps.sem, unit_done(l, u))

            def scaled(dst, bank, factor=1.0):
                return nc.vector.scalar_tensor_tensor(dst, psum[:, bank, :], factor, rnorm[:], ALU.mult, ALU.mult)

            def add_square(l, norm, k, parity):
                wait(dve, sq_ready, l, norm * KT + k)
                nc.vector.tensor_tensor(sq_sum[:], sq_sum[:], tmp[parity][:, 2:], ALU.add).then_inc(sum_step.sem, 1)

            def lo_of_x(l, norm, k, gain):
                wait(dve, xhi_ready, l, norm * KT + k)
                nc.vector.scalar_tensor_tensor(xg_lo[:, k, :], x[:, k, :], gain, xg_hi[:, k, :].bitcast(F32),
                                               ALU.mult, ALU.subtract).then_inc(xlo_ready.sem, 1)

            def mean_square(l, norm):
                wait(dve, sumsq_done, l, norm)
                nc.vector.tensor_scalar(ms[:], psum[:, MS_BANK, 0:TT], 1.0 / D_MODEL, EPS, ALU.mult, ALU.add
                                        ).then_inc(ms_ready.sem, 1)

            def rope_out(l, u):
                dst = qa[:, u, :] if u < 4 else ka[:]
                wait(dve, evac, l, u)
                nc.vector.tensor_tensor(dst, wide[u % 2][:], rope_sb[:, 0, :], ALU.mult).then_inc(rope_mul.sem, 1)
                wait(dve, rot_done, l, u)
                nc.vector.tensor_tensor(wide[2 + u % 2][:], wide[2 + u % 2][:], rope_sb[:, 1, :], ALU.mult
                                        ).then_inc(rope_mul.sem, 1)
                wait(dve, rope_mul, l, 2 * u + 1)
                nc.vector.tensor_tensor(dst, dst, wide[2 + u % 2][:], ALU.add).then_inc(qk_ready.sem, 1)

            def yb_lo(l, c):
                wait(dve, yb_hi_ready, l, c)
                nc.vector.tensor_tensor(ybc_lo[:, c, :], wide[2 + c % 2][:], ybc_hi[:, c, :].bitcast(F32),
                                        ALU.subtract).then_inc(convb.sem, 1)

            def mix_lo_part(l, m):
                wait(dve, mix_hi_ready, l, m)
                nc.vector.scalar_tensor_tensor(mix_lo[:, m, :], merged[:, m, :], 0.5, mix_hi[:, m, :].bitcast(F32),
                                               ALU.mult, ALU.subtract).then_inc(mix_lo_ready.sem, 1)

            def normalise(l, off, h, t):
                n, width = item(off, h, t), len(key_tiles(off, t)) * P
                wait(dve, exp_done, l, n)
                if off == 0:
                    wait(dve, sink_done, l, n)
                    nc.vector.tensor_tensor(denom[:, n:n + 1], denom[:, n:n + 1], sink_e[:, n:n + 1], ALU.add
                                            ).then_inc(denom_done.sem, 1)
                    wait(dve, denom_done, l, n)
                nc.vector.reciprocal(denom[:, n:n + 1], denom[:, n:n + 1]).then_inc(recip_done.sem, 1)
                wait(dve, recip_done, l, n)
                nc.vector.tensor_scalar(prob[t][:, 0:width], prob[t][:, 0:width], denom[:, n:n + 1], None, ALU.mult
                                        ).then_inc(prob_ready.sem, 1)

            def softmax_stage(l, slot):
                stages = head_at(slot)
                if not stages:
                    return
                off, h_s, h_t, h_v = stages
                if h_v is not None and h_v % 2:
                    hi, lo = (ya_hi, ya_lo) if off == 0 else (ybc_hi, ybc_lo)
                    wait(dve, o_hi_ready, l, (off + h_v) // 2)
                    nc.vector.tensor_tensor(lo[:, h_v // 2, :], psum[:, O_BANK, :],
                                            hi[:, h_v // 2, :].bitcast(F32), ALU.subtract).then_inc(o_lo_ready.sem, 1)
                if h_s is not None:
                    for t in range(TT):
                        n, kts = item(off, h_s, t), key_tiles(off, t)
                        width = len(kts) * P
                        if off == 0:
                            head = h_s // 2 + 4 * (h_s % 2)
                            add = mask_a[:, 2 * P - width:]
                            start = neg_sink[:, head:head + 1]
                            if h_s == 0 and t == 0:
                                wait(dve, nsink_ready, l, 0)
                        else:
                            add, start = bias[:, h_s, width - 1::-1], NO_MAX_YET
                        wait(dve, scores_done, l, n)
                        dve.sem_inc(scores_seen, 1)
                        nc.vector.tensor_tensor_reduce(
                            out=prob[t][:, 0:width], in0=psum[:, SCORE_BANK + n % 2, 0:width], in1=add,
                            scale=-1.0, scalar=start, op0=ALU.add, op1=ALU.min,
                            accum_out=neg_max[:, n:n + 1]).then_inc(logits_ready.sem, 1)
                        if t:
                            normalise(l, off, h_s, t - 1)
                    normalise(l, off, h_s, TT - 1)

            rows, near = DEPTH * C_HEADS, CHUNK
            far = REL_EXT - near - C_REL_SIZE
            dve.wait_ge(rel_in, 16)
            nc.vector.tensor_copy(rel_ext[0:rows, 0:near], rel_tab[0:rows, 0:1].to_broadcast([rows, near])
                                  ).then_inc(rel_built, 1)
            nc.vector.tensor_copy(rel_ext[0:rows, near:near + C_REL_SIZE], rel_tab[0:rows, :]).then_inc(rel_built, 1)
            nc.vector.tensor_copy(rel_ext[0:rows, near + C_REL_SIZE:REL_EXT],
                                  rel_tab[0:rows, C_REL_SIZE - 1:C_REL_SIZE].to_broadcast([rows, far])
                                  ).then_inc(rel_built, 1)

            dve.wait_ge(consts_set, 1)
            for k in range(KT):
                lo_of_x(0, 0, k, g0[:, k:k + 1])
            for k in range(KT):
                if k > 2:
                    dve.wait_ge(sum_step.sem, k - 2)
                nc.vector.tensor_tensor(sq_sum[:] if k == 0 else tmp[k % 2][:, 2:], x[:, k, :], x[:, k, :], ALU.mult
                                        ).then_inc(first_squares, 1)
                if k:
                    dve.wait_ge(first_squares, k + 1)
                    if k > 1:
                        wait(dve, sum_step, 0, k - 2)
                    nc.vector.tensor_tensor(sq_sum[:], sq_sum[:], tmp[k % 2][:, 2:], ALU.add).then_inc(sum_step.sem, 1)
            dve.wait_ge(par_in, 16)

            with dve.Fori(0, DEPTH) as l:
                mean_square(l, 0)
                nc.vector.tensor_copy(par[:], par_all[:, bass.ds(l, 1), :].rearrange("p a n -> p (a n)")
                                      ).then_inc(par_ready.sem, 1)
                wait(dve, par_ready, l, 0)
                nc.vector.tensor_scalar(neg_sink[:], par[:, PSK:PSK + A_Q_HEADS], -1.0, None, ALU.mult
                                        ).then_inc(nsink_ready.sem, 1)
                for u in range(U_OUT):
                    outs = unit_outs(u)
                    banks = [o % PROJ_BANKS for o in outs]
                    unit_wait(l, u)
                    if u == 0:
                        wait(dve, rnorm_ready, l, 0)
                        dve.wait_ge(rel_stored, 16)
                        dve.wait_ge(rope_in, l * 16 + 16)
                    if u < 5:
                        scaled(wide[u % 2][:], banks[0], SCALE if u < 4 else 1.0).then_inc(evac.sem, 1)
                        if u:
                            rope_out(l, u - 1)
                    elif u == 5:
                        scaled(tmp[u % 2][:, 2:], banks[0]).then_inc(evac.sem, 1)
                        rope_out(l, 4)
                    elif u < U_C + 4:
                        scaled(qc[:, u - U_C, :], banks[0], SCALE).then_inc(evac.sem, 1)
                    elif u < U_C + 8:
                        scaled(kc[:, u - U_C - 4, :], banks[0]).then_inc(evac.sem, 1)
                    elif u < U_B:
                        scaled(tmp[u % 2][:, 2:], banks[0]).then_inc(evac.sem, 1)
                    elif u < U_MERGE:
                        c, part = divmod(u - U_B, 3)
                        y = wide[2 + c % 2]
                        scaled(wide[(0, 1, 4)[part]][:], banks[0]).then_inc(evac.sem, 1)
                        if part == 0 and c:
                            yb_lo(l, c - 1)
                        if part == 1:
                            wait(dve, evac, l, u)
                            nc.vector.tensor_tensor(tmp[c % 2][:, 2:], wide[0][:], wide[1][:], ALU.mult
                                                    ).then_inc(convb.sem, 1)
                        if part == 2:
                            wait(dve, tapb_done, l, c)
                            for tap in (1, 0):
                                nc.vector.scalar_tensor_tensor(
                                    y[:], tmp[c % 2][:, tap:tap + SEQ], par[:, PCB + 3 * c + tap:PCB + 3 * c + tap + 1],
                                    y[:], ALU.mult, ALU.add).then_inc(convb.sem, 1)
                                wait(dve, convb, l, 5 * c + 2 - tap)
                            wait(dve, evac, l, u)
                            nc.vector.tensor_tensor(y[:], y[:], wide[4][:], ALU.mult).then_inc(convb.sem, 1)
                    else:
                        br, mp, part = merge_group(u)
                        if part < 2:
                            if br == 2 or (br, mp > 0) == (1, True):
                                wait(dve, merged_sum, l, (br - 1) * KT + 2 * mp - 2 + part)
                            scaled(tmp[part][:, 2:], banks[0]).then_inc(evac.sem, 1)
                            if u == U_MERGE:
                                yb_lo(l, 3)
                            if br == 2 and part == 0 and mp:
                                mix_lo_part(l, 2 * mp - 2)
                                mix_lo_part(l, 2 * mp - 1)
                        else:
                            for b, m in enumerate((2 * mp, 2 * mp + 1)):
                                wait(dve, gate_ready, l, br * KT + m)
                                dst = merged[:, m, :] if br == 0 else tmp[b][:, 2:]
                                nc.vector.scalar_tensor_tensor(dst, tmp[2 + b][:, 2:], 1.0, psum[:, banks[b], :],
                                                               ALU.add, ALU.mult).then_inc(evac.sem, 1)
                            for b, m in enumerate((2 * mp, 2 * mp + 1) if br else ()):
                                wait(dve, evac, l, outs[b])
                                nc.vector.tensor_tensor(merged[:, m, :], merged[:, m, :], tmp[b][:, 2:], ALU.add
                                                        ).then_inc(merged_sum.sem, 1)
                            if br == 2 and mp == 3:
                                mix_lo_part(l, 6)
                                mix_lo_part(l, 7)
                    if u == U_MERGE:
                        dve.wait_ge(bias_in, l * 16 + 16)
                        nc.vector.memset(bias[0:HALF, :, 0:CHUNK], MASKED).then_inc(bias_masked, 1)
                        dve.wait_ge(bias_masked, l + 1)
                    softmax_stage(l, u + 1)

                def residual(bank, k):
                    nc.vector.tensor_tensor(x[:, k, :], x[:, k, :], psum[:, bank, :], ALU.add).then_inc(evac.sem, 1)

                for k in range(KT):
                    unit_wait(l, U_OUT + k)
                    residual(k % 4, k)
                    lo_of_x(l, 1, k, par[:, PG2 + k:PG2 + k + 1])
                    if k > 1:
                        wait(dve, sum_step, l, KT - 1 + k - 2)
                    if k:
                        add_square(l, 1, k, k % 2)
                mean_square(l, 1)

                def up_pair(i, b, first=False):
                    g_in_, v_in_, yg, yv, th = tmp[2 * b], tmp[2 * b + 1], wide[2 * b], wide[2 * b + 1], wide[4 + b]
                    for j in range(2):
                        unit_wait(l, i * 4 + (U_UP + 2 * b + j))
                        if first and j == 0:
                            wait(dve, rnorm_ready, l, 1)
                        scaled(tmp[2 * b + j][:, 2:], 2 * b + j).then_inc(evac.sem, 1)
                    for tap in (1, 0):
                        for j, (src, y) in enumerate(((g_in_, yg), (v_in_, yv))):
                            if tap == 1:
                                wait(dve, ff_act, l, 4 * b + j + i * 8)
                                wait(dve, evac, l, O_UP + 2 * b + j + i * 4)
                            else:
                                wait(dve, ff_vec, l, 7 * b + j + i * 14)
                            nc.vector.scalar_tensor_tensor(
                                y[:], src[:, tap:tap + SEQ], par[:, bass.ds(i * 6 + (PCF + 3 * (FF_T * j + b) + tap), 1)],
                                y[:], ALU.mult, ALU.add).then_inc(ff_vec.sem, 1)
                    wait(dve, ff_act, l, 4 * b + 2 + i * 8)
                    wait(dve, ff_vec, l, 7 * b + 3 + i * 14)
                    nc.vector.scalar_tensor_tensor(th[:], th[:], 1.0, yg[:], ALU.add, ALU.mult).then_inc(ff_vec.sem, 1)
                    wait(dve, ff_vec, l, 7 * b + 4 + i * 14)
                    nc.vector.scalar_tensor_tensor(th[:], th[:], 0.5, yv[:], ALU.mult, ALU.mult
                                                   ).then_inc(ff_vec.sem, 1)
                    wait(dve, ff_act, l, 4 * b + 3 + i * 8)
                    at = bass.ds(i * 2 + b, 1)
                    nc.vector.tensor_tensor(ff_lo[:, at, :].rearrange("p a t -> p (a t)"), th[:],
                                            ff_hi[:, at, :].rearrange("p a t -> p (a t)").bitcast(F32),
                                            ALU.subtract).then_inc(ff_vec.sem, 1)

                up_pair(0, 0, first=True)
                up_pair(0, 1)
                with dve.Fori(1, FF_T // 2) as i:
                    up_pair(i, 0)
                    up_pair(i, 1)

                for k in range(KT):
                    unit_wait(l, U_DOWN + (k * FF_T + FF_T - 1) // TILES)
                    residual(k % 4, k)

                    def add():
                        if k > 1:
                            wait(dve, sum_step, l + 1, k - 2)
                        if k:
                            add_square(l + 1, 0, k, k % 2)
                    if k == KT - 1:
                        add()
                    lo_of_x(l + 1, 0, k, par[:, PGN + k:PGN + k + 1])
                    if k < KT - 1:
                        add()
            mean_square(DEPTH, 0)
            wait(dve, rnorm_ready, DEPTH, 0)
            for k in range(KT):
                nc.vector.scalar_tensor_tensor(x_out[:, k, :], x[:, k, :], par[:, PGN + k:PGN + k + 1], rnorm[:],
                                               ALU.mult, ALU.mult).then_inc(out_ready, 1)


def _units(w_in, w_o_a, w_o_b, w_o_c, w_out, w_up, w_down):
    heads = [h for j in range(PAIRS) for h in (j, j + A_Q_HEADS // A_KV_HEADS)]
    pair_rows = np.concatenate([np.arange(h * HEAD_DIM, (h + 1) * HEAD_DIM) for h in heads])
    stream = []
    for l in range(DEPTH):
        def tile(w, k, m):
            return w[k * P:(k + 1) * P, m * P:(m + 1) * P]

        def column(w, m):
            return [tile(w, k, m) for k in range(KT)]

        cols = np.arange(w_in.shape[2])
        at = np.cumsum([0, 512, 128, 128, 512, 512, 512, 512, 512, 512])
        cols[0:512] = pair_rows
        w = w_in[l][:, cols]
        q_a, k_a, v_a, b_b, c_b, u_b, q_c, k_c, v_c, gate = (int(c) // P for c in at)
        tiles = []
        for m in list(range(q_a, q_a + 4)) + [k_a, v_a] + list(range(q_c, q_c + 12)):
            tiles += column(w, m)
        for c in range(4):
            for m in (u_b + c, c_b + c, b_b + c):
                tiles += column(w, m)
        for branch, w_o in ((1, w_o_b[l]), (0, w_o_a[l][pair_rows]), (2, w_o_c[l])):
            for m in range(0, KT, 2):
                tiles += column(w, gate + branch * KT + m) + column(w, gate + branch * KT + m + 1)
                tiles += [tile(w_o, k, n) for n in (m, m + 1) for k in range(4)]
        for m in range(KT):
            tiles += column(w_out[l], m)
        for m in range(FF_T):
            tiles += column(w_up[l], m) + column(w_up[l], FF_T + m)
        tiles += [tile(w_down[l], k, m) for m in range(KT) for k in range(FF_T)]
        stream += tiles
    a = np.stack(stream).reshape(DEPTH * UNITS, TILES, P, P)
    return np.ascontiguousarray(a.transpose(0, 2, 1, 3)).reshape(DEPTH * UNITS, P, TILES * P)


def _by_feature(v):
    return np.moveaxis(v.reshape(v.shape[:-1] + (-1, P)), -1, 0)


def _rope_tables():
    half = HEAD_DIM // 2
    inv = np.float32(ROPE_THETA) ** (-np.arange(half, dtype=np.float32) / np.float32(half))
    angle = (np.arange(SEQ, dtype=np.float32)[None, :] * inv[:, None]).astype(np.float32)
    cos, sin = np.cos(angle), np.sin(angle)
    return np.stack([np.tile(cos, (4, 1)), np.concatenate([-sin, sin, -sin, sin])], axis=1).astype(np.float32)


def kernel(**inputs):
    import concourse.bacc as bacc
    from concourse.bass_utils import run_bass_kernel_spmd

    a = {name: np.asarray(v) for name, v in inputs.items()}
    g1 = [_by_feature(a["mix_norm_g"][l]) for l in range(DEPTH)] + [_by_feature(a["final_norm_g"])]
    params = []
    for l in range(DEPTH):
        conv_b = _by_feature(a["conv_b_w"][l])
        conv_f = _by_feature(a["ffn_conv_w"][l])
        params.append(np.concatenate([
            _by_feature(a["ffn_norm_g"][l]), g1[l + 1],
            conv_b.transpose(0, 2, 1).reshape(P, -1), conv_f.transpose(0, 2, 1).reshape(P, -1),
            np.broadcast_to(a["attn_sinks"][l], (P, A_Q_HEADS))], axis=1))
    arrays = {
        "xT": np.ascontiguousarray(a["x"][0].T),
        "weights": _units(*(a[n] for n in ("w_in", "w_o_a", "w_o_b", "w_o_c", "w_out", "w_up", "w_down"))),
        "g_first": np.ascontiguousarray(g1[0]),
        "params": np.ascontiguousarray(np.stack(params)),
        "rope": _rope_tables(),
        "rel": np.ascontiguousarray(a["rel_bias"].reshape(DEPTH * C_HEADS, C_REL_SIZE)),
    }
    nc = bacc.Bacc("TRN2", target_bir_lowering=False, num_devices=1)
    drams = [nc.dram_tensor(name, v.shape, mybir.dt.from_np(v.dtype), kind="ExternalInput").ap()
             for name, v in arrays.items()]
    out = nc.dram_tensor("outT", (D_MODEL, SEQ), F32, kind="ExternalOutput").ap()
    build_trunk(nc, *drams, out)
    r = run_bass_kernel_spmd(nc, [arrays], core_ids=[0])
    return np.ascontiguousarray(r.results[0]["outT"].T)[None]
```

```python
from contextlib import ExitStack

import numpy as np

import concourse.bass as bass
from concourse import mybir

F32 = mybir.dt.float32
F32R = mybir.dt.float32r
ALU = mybir.AluOpType
ACT = mybir.ActivationFunctionType

P = 128
D_MODEL = 1024
SEQ = 512
DEPTH = 2
CHUNK = 64
HEAD_DIM = 64
A_Q_HEADS = 8
A_KV_HEADS = 2
B_CHANNELS = 512
C_HEADS = 8
C_REL_MAX = 256
C_REL_SIZE = CHUNK + C_REL_MAX
D_FF = 2816
TAPS = 3
ROPE_THETA = 10000.0
EPS = 1e-6
MASKED = -1e30
NO_MAX_YET = 3e38

KT = D_MODEL // P
TT = SEQ // P
HALF = P // 2
PAIRS = 4
FF_T = D_FF // P
SCALE = HEAD_DIM ** -0.5

TILES = 8
U_A = 0
U_C = U_A + 6
U_B = U_C + 12
U_MERGE = U_B + 12
U_OUT = U_MERGE + 36
U_UP = U_OUT + KT
U_DOWN = U_UP + 2 * FF_T
UNITS = U_DOWN + FF_T * KT // TILES
assert UNITS % 4 == 0 and U_OUT % 2 == 0 and U_UP % 2 == 0
RAW_SLOTS, HI_SLOTS, LO_SLOTS = 4, 2, 2
FIRST_HI = HI_SLOTS
POOL_OUT = 5

PROJ_BANKS = 3
SCORE_BANK, PT_BANK, O_BANK = 3, 5, 7
MS_BANK, RB_BANK = 5, 6

O_OUT = U_MERGE + 3 * 2 * KT
O_UP = O_OUT + KT
O_DOWN = O_UP + 2 * FF_T
OUTS = O_DOWN + KT

A_START = U_C + 1
C_START = U_MERGE + 14

PG2, PGN, PCB, PCF = 0, KT, 2 * KT, 2 * KT + 4 * TAPS
PSK = PCF + 2 * FF_T * TAPS
NPAR = PSK + A_Q_HEADS

REL_EXT = 2 * SEQ


class Tally:

    def __init__(self, sem, per_layer, credit=0):
        self.sem, self.per_layer, self.credit = sem, per_layer, credit

    def after(self, l, n):
        return l * self.per_layer + (n + (1 + self.credit))


def merge_group(u):
    g, part = divmod(u - U_MERGE, 3)
    return g // 4, g % 4, part


def unit_outs(u):
    if u < U_MERGE:
        return [u]
    g, part = divmod(u - U_MERGE, 3)
    first = U_MERGE + 4 * g
    return [[first], [first + 1], [first + 2, first + 3]][part]


def head_at(slot):
    for off, start in ((0, A_START), (8, C_START)):
        h = slot - start
        if 0 <= h < 8 + 2:
            return off, (h if h < 8 else None), (h - 1 if 0 <= h - 1 < 8 else None), (h - 2 if 0 <= h - 2 < 8 else None)
    return None


def split_head(slot):
    for off, start in ((0, A_START), (8, C_START)):
        if 0 <= slot + 1 - start < 8:
            return off, slot + 1 - start
    return None


def item(off, h, t):
    return (off + h) * TT + t


def key_tiles(off, t):
    return list(range(max(t - 1, 0), t + 1)) if off == 0 else list(range(t + 1))


def seen(off, t):
    end = len(key_tiles(off, t)) * P
    return slice(CHUNK if off == 0 and t else 0, end)


def build_trunk(nc, xT, weights, g_first, params, rope, rel, outT):
    ctx = ExitStack()
    with ctx:
        def sb(name, shape, dt=F32):
            return ctx.enter_context(nc.sbuf_tensor(name, shape, dt))

        def sem(name):
            return ctx.enter_context(nc.semaphore(name))

        rel_ext_dram = nc.dram_tensor("rel_ext_dram", [DEPTH * C_HEADS, REL_EXT], F32, kind="Internal").ap()

        x = sb("x", [P, KT, SEQ])
        xg_hi = sb("xg_hi", [P, KT, SEQ], F32R)
        xg_lo = sb("xg_lo", [P, KT, SEQ], F32R)
        rnorm = sb("rnorm", [P, SEQ])
        sq_sum = sb("sq_sum", [P, SEQ])
        raw = sb("raw", [P, RAW_SLOTS, TILES * P])
        w_hi = sb("w_hi", [P, HI_SLOTS, TILES * P], F32R)
        w_lo = sb("w_lo", [P, LO_SLOTS, TILES * P], F32R)
        par_all = sb("par_all", [P, DEPTH, NPAR])
        par = sb("par", [P, NPAR])
        g0 = sb("g0", [P, KT])
        q_split = sb("q_split", [P, 2, SEQ], F32R)
        k_twice = sb("k_twice", [P, 2, SEQ], F32R)
        k_lo = sb("k_lo", [P, SEQ], F32R)
        neg_sink = sb("neg_sink", [P, A_Q_HEADS])
        ident = sb("ident", [P, P])
        ones = sb("ones", [P, 1])
        minus_half = sb("minus_half", [P, TT])
        ms = sb("ms", [P, TT])
        r_tok = sb("r_tok", [P, TT])
        mask_a = sb("mask_a", [P, 2 * P])
        neg_max = sb("neg_max", [P, 16 * TT])
        denom = sb("denom", [P, 16 * TT])
        sink_e = sb("sink_e", [P, 8 * TT])
        tmp = [sb(f"tmp{i}", [P, SEQ + 2]) for i in range(4)]

        sb("zone", [P, 44 * SEQ])
        zone_at = nc.sbuf_base - 4 * 44 * SEQ
        sb("soft", [P, 1280 + TT * SEQ])
        soft_at = nc.sbuf_base - 4 * (1280 + TT * SEQ)

        def view(name, base, start, shape, dt=F32):
            return nc.alloc_sbuf_tensor_at(name, [P] + shape, dt, offset=base + 4 * start)

        T = SEQ
        qa = view("qa", zone_at, 0, [PAIRS, T])
        ka = view("ka", zone_at, 4 * T, [T])
        va = view("va", zone_at, 5 * T, [TT, P])
        rope_sb = view("rope_sb", zone_at, 6 * T, [2, T])
        merged = view("merged", zone_at, 0, [KT, T])
        qc = view("qc", zone_at, 8 * T, [PAIRS, T])
        kc = view("kc", zone_at, 12 * T, [PAIRS, T])
        vc = view("vc", zone_at, 16 * T, [TT, T])
        bias = view("bias", zone_at, 20 * T, [C_HEADS, T])
        mix_hi = view("mix_hi", zone_at, 8 * T, [KT, T], F32R)
        mix_lo = view("mix_lo", zone_at, 16 * T, [KT, T], F32R)
        ya_hi = view("ya_hi", zone_at, 28 * T, [PAIRS, T], F32R)
        ya_lo = view("ya_lo", zone_at, 32 * T, [PAIRS, T], F32R)
        ybc = view("ybc", zone_at, 36 * T, [PAIRS, 2, T], F32R)
        ybc_hi, ybc_lo = ybc[:, :, 0, :], ybc[:, :, 1, :]
        ff_hi = view("ff_hi", zone_at, 0, [FF_T, T], F32R)
        ff_lo = view("ff_lo", zone_at, FF_T * T, [FF_T, T], F32R)
        prob = [view(f"prob{t}", soft_at, 64 * t * (t + 1), [(t + 1) * P]) for t in range(TT)]
        prob_t_soft = view("prob_t_soft", soft_at, 1280, [TT * T])
        prob_t_ybc = view("prob_t_ybc", zone_at, 42 * T, [2 * T])
        wide = [view(f"wide{i}", soft_at, T * i, [T]) for i in range(6)]
        x_out = view("x_out", zone_at, 0, [KT, T])
        rel_tab = view("rel_tab", soft_at, 0, [C_REL_SIZE])
        rel_ext = view("rel_ext", soft_at, T, [REL_EXT])

        psum = ctx.enter_context(nc.psum_tensor("psum", [P, 8, SEQ], F32))

        raw_in = [sem(f"raw_in{i}") for i in range(RAW_SLOTS)]
        x_in = [sem(f"x_in{i}") for i in range(4)]
        g_in, par_in, rope_in, rel_in, bias_in = (sem(n) for n in ("g_in", "par_in", "rope_in", "rel_in", "bias_in"))
        rel_built, rel_stored, out_stored = sem("rel_built"), sem("rel_stored"), sem("out_stored")
        ident_set, consts_set, bias_masked, scores_seen = sem("ident_set"), sem("consts_set"), sem("bias_masked"), sem("scores_seen")
        zeros_set = sem("zeros_set")
        unit_steps = Tally(sem("unit_steps"), 2 * UNITS, 2 * HI_SLOTS)
        scores_done = Tally(sem("scores_done"), 16 * TT)
        probt_done = Tally(sem("probt_done"), 16 * TT)
        vt_done = Tally(sem("vt_done"), 5)
        pv_done = Tally(sem("pv_done"), 8)
        sumsq_done = Tally(sem("sumsq_done"), 2)
        rb_done = Tally(sem("rb_done"), 2)
        x_gained = sem("x_gained")
        hi_ready = Tally(sem("hi_ready"), UNITS - FIRST_HI, -FIRST_HI)
        xhi_ready = Tally(sem("xhi_ready"), 2 * KT)
        sq_ready = Tally(sem("sq_ready"), 2 * KT)
        rnorm_ready = Tally(sem("rnorm_ready"), 2)
        rot_done = Tally(sem("rot_done"), 5)
        v_ready = Tally(sem("v_ready"), 5)
        tapb_done = Tally(sem("tapb_done"), 4)
        yb_hi_ready = Tally(sem("yb_hi_ready"), 4)
        qk_hi_ready = Tally(sem("qk_hi_ready"), 16)
        exp_done = Tally(sem("exp_done"), 16 * TT)
        sink_done = Tally(sem("sink_done"), 8 * TT)
        probt_ready = Tally(sem("probt_ready"), 16 * TT)
        o_hi_ready = Tally(sem("o_hi_ready"), 8)
        gate_ready = Tally(sem("gate_ready"), 3 * KT)
        mix_hi_ready = Tally(sem("mix_hi_ready"), KT)
        ff_act = Tally(sem("ff_act"), 4 * FF_T)
        evac = Tally(sem("evac"), OUTS, 4)
        xlo_ready = Tally(sem("xlo_ready"), 2 * KT)
        sum_step = Tally(sem("sum_step"), 2 * (KT - 1))
        ms_ready = Tally(sem("ms_ready"), 2)
        par_ready = Tally(sem("par_ready"), 1)
        nsink_ready = Tally(sem("nsink_ready"), 1)
        rope_mul = Tally(sem("rope_mul"), 10)
        qk_ready = Tally(sem("qk_ready"), 5)
        convb = Tally(sem("convb"), 20)
        qk_lo_ready = Tally(sem("qk_lo_ready"), 16)
        logits_ready = Tally(sem("logits_ready"), 16 * TT)
        denom_done = Tally(sem("denom_done"), 8 * TT)
        recip_done = Tally(sem("recip_done"), 16 * TT)
        prob_ready = Tally(sem("prob_ready"), 16 * TT)
        o_lo_ready = Tally(sem("o_lo_ready"), 8)
        merged_sum = Tally(sem("merged_sum"), 2 * KT)
        mix_lo_ready = Tally(sem("mix_lo_ready"), KT)
        ff_vec = Tally(sem("ff_vec"), 7 * FF_T)
        out_ready = sem("out_ready")
        first_hi_ready = Tally(sem("first_hi_ready"), FIRST_HI)
        lo_ready = Tally(sem("lo_ready"), UNITS, RAW_SLOTS)
        out_ready_pool = sem("out_ready_pool")
        rtok_ready = Tally(sem("rtok_ready"), 2)

        def prob_t(h, kts, q, nq):
            if h % 2 == 0:
                at, first, step = prob_t_soft, 0, 3 * P
            elif kts[-1] < 2:
                at, first, step = prob_t_ybc, 0, 3 * P
            else:
                at, first, step = prob_t_soft, 13 * P - 4 * P, P
            start = first + kts[0] * step + q
            if len(kts) == 1:
                return at[:, start:start + nq]
            origin = at[:, start:start + nq]
            return bass.AP(tensor=origin.tensor, offset=origin.offset,
                           ap=[origin.ap[0], [step, len(kts)], origin.ap[1]])

        def head_rows(off, h):
            own, other = HALF * (h % 2), HALF * (1 - h % 2)
            own, other = slice(own, own + HALF), slice(other, other + HALF)
            return own, other, (qa if off == 0 else qc)[own, h // 2, :], ka[own, :] if off == 0 else kc[own, h // 2, :]

        def hi_used(l, u):
            return unit_steps.after(l, 2 * u)

        def unit_done(l, u):
            return unit_steps.after(l, 2 * u + 1)

        def wait(eng, tally, l, n):
            eng.wait_ge(tally.sem, tally.after(l, n))

        def hi_wait(eng, l, u):
            if isinstance(u, int) and u < FIRST_HI:
                wait(eng, first_hi_ready, l, u)
            else:
                wait(eng, hi_ready, l, u)

        def load_x(eng, i):
            eng.dma_start(x[:, 2 * i:2 * i + 2, :], xT.rearrange("(k p) t -> p k t", p=P)[:, 2 * i:2 * i + 2, :]
                          ).then_inc(x_in[i], 16)

        block = ctx.enter_context(nc.Block())

        @block.sync
        def _(sp):
            def load_units(l, quad):
                for slot in range(RAW_SLOTS):
                    u = quad * RAW_SLOTS + slot
                    sp.wait_ge(lo_ready.sem, lo_ready.after(l, u - RAW_SLOTS))
                    if isinstance(u, int) and u == 1:
                        sp.wait_ge(x_in[2], 16)
                    sp.dma_start(raw[:, slot, :],
                                 weights[bass.ds(l * UNITS + u, 1)].rearrange("a p n -> p (a n)")
                                 ).then_inc(raw_in[slot], 16)

            def load_rope(l):
                sp.wait_ge(unit_steps.sem, unit_steps.after(l, -1))
                sp.dma_start(rope_sb[:], rope).then_inc(rope_in, 16)

            def load_bias(l):
                sp.wait_ge(rel_stored, 16)
                rows = bass.AP(tensor=rel_ext_dram.tensor, offset=0,
                               ap=[[C_HEADS * REL_EXT, DEPTH], [1, P], [REL_EXT, C_HEADS], [1, SEQ]])
                sp.dma_start(bias[:], rows[bass.ds(l, 1)].rearrange("a p h n -> (a p) h n")).then_inc(bias_in, 16)

            load_x(sp, 0)
            with sp.Fori(0, DEPTH) as l:
                load_units(l, 0)
                load_rope(l)
                with sp.Fori(1, U_B // RAW_SLOTS + 1) as q:
                    load_units(l, q)
                load_bias(l)
                with sp.Fori(U_B // RAW_SLOTS + 1, UNITS // RAW_SLOTS) as q:
                    load_units(l, q)
            for k in (0, 1, 5, 2, 3, 6, 4, 7):
                if k < POOL_OUT:
                    sp.wait_ge(out_ready, k + 1)
                else:
                    sp.wait_ge(out_ready_pool, k - POOL_OUT + 1)
                sp.dma_start(outT.rearrange("(k p) t -> p k t", p=P)[:, k, :],
                             x_out[:, k, :]).then_inc(out_stored, 16)
            sp.wait_ge(out_stored, 16 * KT)

        @block.gpsimd
        def _(pool):
            pool.sem_inc(lo_ready.sem, lo_ready.credit)
            nc.gpsimd.memset(ident[:], 0.0).then_inc(zeros_set, 1)
            pool.wait_ge(zeros_set, 1)
            nc.gpsimd.affine_select(out=ident[:], in_=ident[:], compare_op=ALU.not_equal, fill=1.0, base=0,
                                    pattern=[[-1, P]], channel_multiplier=1).then_inc(ident_set, 1)

            def lo_part(l, u, raw_slot):
                hi_wait(pool, l, u)
                pool.wait_ge(unit_steps.sem, unit_done(l, u - LO_SLOTS))
                slot = raw_slot % 2
                nc.gpsimd.tensor_tensor(w_lo[:, slot, :], raw[:, raw_slot, :],
                                        w_hi[:, slot, :].bitcast(F32), ALU.subtract).then_inc(lo_ready.sem, 1)

            def first_hi_part(l, u):
                pool.wait_ge(unit_steps.sem, hi_used(l, u - HI_SLOTS))
                wait(pool, lo_ready, l, u - HI_SLOTS)
                pool.wait_ge(raw_in[u], l * (16 * (UNITS // RAW_SLOTS)) + 16)
                nc.gpsimd.tensor_tensor(w_hi[:, u, :], raw[:, u, :], ones[:, 0:1].to_broadcast([P, TILES * P]),
                                        ALU.mult).then_inc(first_hi_ready.sem, 1)

            def row_factors(l, norm):
                wait(pool, ms_ready, l, norm)
                nc.gpsimd.tensor_tensor(r_tok[:], ms[:], minus_half[:], ALU.pow).then_inc(rtok_ready.sem, 1)

            pool.wait_ge(consts_set, 1)
            with pool.Fori(0, DEPTH) as l:
                for u in range(FIRST_HI):
                    first_hi_part(l, u)
                    lo_part(l, u, u)
                row_factors(l, 0)
                with pool.Fori(0, (U_UP - 2) // 4) as q:
                    for j in range(2, 6):
                        lo_part(l, q * 4 + j, j % 4)
                lo_part(l, U_UP, U_UP % 4)
                lo_part(l, U_UP + 1, (U_UP + 1) % 4)
                row_factors(l, 1)
                with pool.Fori((U_UP + 2) // 4, UNITS // 4) as q:
                    for j in range(4):
                        lo_part(l, q * 4 + j, j)
            row_factors(DEPTH, 0)
            pool.wait_ge(x_gained, KT - POOL_OUT)
            wait(pool, rnorm_ready, DEPTH, 0)
            for k in range(POOL_OUT, KT):
                nc.gpsimd.tensor_tensor(x_out[:, k, :], x_out[:, k, :], rnorm[:], ALU.mult).then_inc(out_ready_pool, 1)

        @block.scalar
        def _(act):
            def hi_part(l, u, raw_slot):
                act.wait_ge(unit_steps.sem, hi_used(l, u - HI_SLOTS))
                wait(act, lo_ready, l, u - HI_SLOTS)
                act.wait_ge(raw_in[raw_slot], l * (16 * (UNITS // 4)) + (u - raw_slot) * 4 + 16)
                nc.scalar.copy(w_hi[:, raw_slot % 2, :], raw[:, raw_slot, :]).then_inc(hi_ready.sem, 1)

            def hi_of_x(k, gain):
                nc.scalar.activation(xg_hi[:, k, :], x[:, k, :], ACT.Identity, scale=gain).then_inc(xhi_ready.sem, 1)

            def square(k):
                nc.scalar.activation(sq_sum[:] if k == 0 else tmp[k % 2][:, 2:], x[:, k, :], ACT.Square
                                     ).then_inc(sq_ready.sem, 1)

            def split_x(norm, k, gain):
                if (norm, k) == (0, KT - 1):
                    square(k)
                    hi_of_x(k, gain)
                else:
                    hi_of_x(k, gain)
                    square(k)

            def row_factor_out(l, norm):
                wait(act, rb_done, l, norm)
                nc.scalar.copy(rnorm[:], psum[:, RB_BANK, :]).then_inc(rnorm_ready.sem, 1)

            def rotate(l, u):
                wait(act, evac, l, u)
                for q in range(4):
                    r = nc.scalar.copy(wide[2 + u % 2][32 * q:32 * q + 32, :],
                                       wide[u % 2][32 * (q ^ 1):32 * (q ^ 1) + 32, :])
                r.then_inc(rot_done.sem, 1)

            def split_qk_hi(l, slot):
                if not split_head(slot):
                    return
                off, h = split_head(slot)
                own, other, q, k = head_rows(off, h)
                if h == 0:
                    if off == 0:
                        wait(act, qk_ready, l, 4)
                    else:
                        wait(act, evac, l, U_C + 7)
                if off or h > 1:
                    wait(act, scores_done, l, item(off, h, TT - 1) - 2 * TT)
                if off or h < 2:
                    nc.scalar.copy(k_twice[own, h % 2, :], k)
                    nc.scalar.copy(k_twice[other, h % 2, :], k)
                nc.scalar.copy(q_split[own, h % 2, :], q).then_inc(qk_hi_ready.sem, 1)

            def gate(l, u):
                part = merge_group(u)[2]
                wait(act, evac, l, unit_outs(u)[0])
                nc.scalar.activation(tmp[2 + part][:, 2:], tmp[part][:, 2:], ACT.Tanh, scale=0.5
                                     ).then_inc(gate_ready.sem, 1)

            def softmax_stage(l, slot, gate_of):
                stages = head_at(slot)
                if not stages:
                    if gate_of is not None:
                        gate(l, gate_of)
                    split_qk_hi(l, slot)
                    return
                off, h_s, h_t, h_v = stages
                if h_v is not None and h_v % 2:
                    pair = (off + h_v) // 2
                    hi = ya_hi if off == 0 else ybc_hi
                    wait(act, pv_done, l, pair)
                    nc.scalar.copy(hi[:, h_v // 2, :], psum[:, O_BANK, :]).then_inc(o_hi_ready.sem, 1)
                for t in range(TT):
                    if t == 2:
                        split_qk_hi(l, slot)
                    if h_t is not None:
                        n, kts = item(off, h_t, t), key_tiles(off, t)
                        wait(act, probt_done, l, n)
                        parts = [[k for k in kts if k < 2], [k for k in kts if k >= 2]] if h_t % 2 else [kts]
                        for part in filter(None, parts):
                            at = (part[0] - kts[0]) * P
                            src = psum[:, PT_BANK + n % 2, at:at + len(part) * P]
                            if len(part) > 1:
                                src = src.rearrange("p (k q) -> p k q", q=P)
                            m = nc.scalar.copy(prob_t(h_t, part, t * P, P), src)
                        m.then_inc(probt_ready.sem, 1)
                    if h_s is not None:
                        n, cols = item(off, h_s, t), seen(off, t)
                        wait(act, logits_ready, l, n)
                        nc.scalar.activation(prob[t][:, cols], prob[t][:, cols], ACT.Exp, scale=-1.0,
                                             bias=neg_max[:, n:n + 1], accum_out=denom[:, n:n + 1]
                                             ).then_inc(exp_done.sem, 1)
                        if off == 0:
                            head = h_s // 2 + 4 * (h_s % 2)
                            nc.scalar.activation(sink_e[:, n:n + 1], neg_sink[:, head:head + 1], ACT.Exp, scale=-1.0,
                                                 bias=neg_max[:, n:n + 1]).then_inc(sink_done.sem, 1)
                if gate_of is not None:
                    gate(l, gate_of)

            act.dma_start(g0[:], g_first).then_inc(g_in, 16)
            act.dma_start(rel_tab[0:DEPTH * C_HEADS, :], rel).then_inc(rel_in, 16)
            for i in range(1, 4):
                load_x(act, i)
            act.dma_start(par_all[:], params.rearrange("l p n -> p l n")).then_inc(par_in, 16)
            act.wait_ge(g_in, 16)
            for k in range(KT):
                act.wait_ge(x_in[k // 2], 16)
                hi_of_x(k, g0[:, k:k + 1])
            act.wait_ge(rel_built, 3)
            act.dma_start(rel_ext_dram, rel_ext[0:DEPTH * C_HEADS, :]).then_inc(rel_stored, 16)
            for k in range(KT):
                if k > 2:
                    act.wait_ge(sum_step.sem, k - 2)
                square(k)
            with act.Fori(0, DEPTH) as l:
                for u in range(U_OUT):
                    hi_part(l, u + HI_SLOTS, (u + HI_SLOTS) % 4)
                    if u == 1:
                        row_factor_out(l, 0)
                        rotate(l, 0)
                    if 1 <= u < 5:
                        rotate(l, u)
                    if u == U_C + 0 or U_C + 9 <= u < U_C + 13:
                        m = 0 if u == U_C else u - (U_C + 9) + 1
                        wait(act, vt_done, l, m)
                        if m == 0:
                            nc.scalar.copy(va[:], psum[:, PT_BANK, :].rearrange("p (t f) -> p t f", f=P)
                                           ).then_inc(v_ready.sem, 1)
                        else:
                            nc.scalar.copy(vc[:, :, (m - 1) * P:m * P],
                                           psum[:, SCORE_BANK + m % 2, :].rearrange("p (t f) -> p t f", f=P)
                                           ).then_inc(v_ready.sem, 1)
                    if U_B <= u < U_MERGE:
                        c, part = divmod(u - U_B, 3)
                        if part == 1:
                            wait(act, convb, l, 5 * c)
                            nc.scalar.activation(wide[2 + c % 2][:], tmp[c % 2][:, 2:], ACT.Identity,
                                                 scale=par[:, PCB + 3 * c + 2:PCB + 3 * c + 3]
                                                 ).then_inc(tapb_done.sem, 1)
                        if part == 2:
                            wait(act, convb, l, 5 * c + 3)
                            nc.scalar.copy(ybc_hi[:, c, :], wide[2 + c % 2][:]).then_inc(yb_hi_ready.sem, 1)
                    if U_MERGE <= u < U_OUT:
                        br, mp, part = merge_group(u)
                        if part == 2 and br == 2:
                            for m in (2 * mp, 2 * mp + 1):
                                wait(act, merged_sum, l, KT + m)
                                nc.scalar.activation(mix_hi[:, m, :], merged[:, m, :], ACT.Identity, scale=0.5
                                                     ).then_inc(mix_hi_ready.sem, 1)
                    softmax_stage(l, u + 1, gate_of=u if U_MERGE <= u and merge_group(u)[2] < 2 else None)
                for k in range(KT):
                    hi_part(l, U_OUT + HI_SLOTS + k, (U_OUT + HI_SLOTS + k) % 4)
                    wait(act, evac, l, O_OUT + k)
                    split_x(1, k, par[:, PG2 + k:PG2 + k + 1])

                def up_pair(i, b, first=False):
                    for j in range(2):
                        hi_part(l, U_UP + HI_SLOTS + 2 * b + j + i * 4, (U_UP + HI_SLOTS + 2 * b + j) % 4)
                        if first and j == 0:
                            row_factor_out(l, 1)
                        wait(act, evac, l, O_UP + 2 * b + j + i * 4)
                        nc.scalar.activation(wide[2 * b + j][:], tmp[2 * b + j][:, 2:], ACT.Identity,
                                             scale=par[:, bass.ds(i * 6 + (PCF + 3 * (FF_T * j + b) + 2), 1)]
                                             ).then_inc(ff_act.sem, 1)
                    wait(act, ff_vec, l, 7 * b + 2 + i * 14)
                    nc.scalar.activation(wide[4 + b][:], wide[2 * b][:], ACT.Tanh, scale=0.5).then_inc(ff_act.sem, 1)
                    wait(act, ff_vec, l, 7 * b + 5 + i * 14)
                    nc.scalar.copy(ff_hi[:, bass.ds(i * 2 + b, 1), :].rearrange("p a t -> p (a t)"), wide[4 + b][:]
                                   ).then_inc(ff_act.sem, 1)

                up_pair(0, 0, first=True)
                up_pair(0, 1)
                with act.Fori(1, FF_T // 2) as i:
                    up_pair(i, 0)
                    up_pair(i, 1)
                for u in range(U_DOWN, UNITS):
                    if u + HI_SLOTS < UNITS:
                        hi_part(l, u + HI_SLOTS, (u + HI_SLOTS) % 4)
                    for k in range(KT):
                        if (k * FF_T + FF_T - 1) // TILES == u - U_DOWN:
                            wait(act, evac, l, O_DOWN + k)
                            split_x(0, k, par[:, PGN + k:PGN + k + 1])
            for k in range(POOL_OUT, KT):
                nc.scalar.activation(x_out[:, k, :], x[:, k, :], ACT.Identity, scale=par[:, PGN + k:PGN + k + 1]
                                     ).then_inc(x_gained, 1)
            row_factor_out(DEPTH, 0)

        @block.tensor
        def _(pe):
            pe.sem_inc(unit_steps.sem, unit_steps.credit)
            pe.wait_ge(consts_set, 1)
            pe.wait_ge(ident_set, 1)

            def weight_unit(l, u, slot, tiles, before=None, gap=None, late=0):
                hi_wait(pe, l, u)
                m = [None] * 2
                early, last_ones = range(TILES - late), range(TILES - late, TILES)

                def with_w_hi(some):
                    for i in some:
                        dst, a_hi, a_lo, first, _ = tiles[i]
                        if gap and i in (0, 3, 6):
                            gap(i // 3)
                        if before:
                            before(i)
                        w = w_hi[:, slot, i * P:(i + 1) * P]
                        nc.tensor.matmul(dst, w, a_hi, start=first, stop=False)
                        m[0] = nc.tensor.matmul(dst, w, a_lo, start=False, stop=False)

                def with_w_lo(some):
                    for i in some:
                        dst, a_hi, _, _, last = tiles[i]
                        m[1] = nc.tensor.matmul(dst, w_lo[:, slot, i * P:(i + 1) * P], a_hi, start=False, stop=last)

                with_w_hi(early)
                if late:
                    wait(pe, lo_ready, l, u)
                    with_w_lo(early)
                    with_w_hi(last_ones)
                m[0].then_inc(unit_steps.sem, 1)
                if gap:
                    gap(3)
                if late:
                    with_w_lo(last_ones)
                else:
                    wait(pe, lo_ready, l, u)
                    with_w_lo(early)
                m[1].then_inc(unit_steps.sem, 1)

            def x_tiles(bank):
                return [(psum[:, bank, :], xg_hi[:, k, :], xg_lo[:, k, :], k == 0, k == KT - 1) for k in range(KT)]

            def x_waits(l, norm):
                def before(k):
                    wait(pe, xhi_ready, l, norm * KT + k)
                    wait(pe, xlo_ready, l, norm * KT + k)
                return before

            def sum_squares(l, norm):
                wait(pe, sum_step, l, (norm + 1) * (KT - 1) - 1)
                for t in range(TT):
                    m = nc.tensor.matmul(psum[:, MS_BANK, t:t + 1], sq_sum[:, t * P:(t + 1) * P], ones[:],
                                         start=True, stop=True)
                m.then_inc(sumsq_done.sem, 1)

            def spread_row_factors(l, norm):
                wait(pe, rtok_ready, l, norm)
                for t in range(TT):
                    m = nc.tensor.matmul(psum[:, RB_BANK, t * P:(t + 1) * P],
                                         r_tok[:, t:t + 1].to_broadcast([P, P]), ident[:], start=True, stop=True)
                m.then_inc(rb_done.sem, 1)

            def scores(l, off, h, t):
                n, kts = item(off, h, t), key_tiles(off, t)
                cols, queries = seen(off, t), slice(t * P, (t + 1) * P)
                keys = slice(kts[0] * P + cols.start, kts[0] * P + cols.stop)
                own = head_rows(off, h)[0]
                if t == 0:
                    wait(pe, qk_lo_ready, l, off + h)
                    if off and h == 0:
                        wait(pe, v_ready, l, 4)
                if t >= 2 or h > 0:
                    wait(pe, logits_ready, l, n - 2)
                dst = psum[:, SCORE_BANK + n % 2, cols]
                nc.tensor.matmul(dst, q_split[:, h % 2, queries], k_twice[:, h % 2, keys], start=True, stop=False)
                m = nc.tensor.matmul(dst, q_split[own, h % 2, queries], k_lo[own, keys], start=False, stop=True)
                m.then_inc(scores_done.sem, 1)

            def transpose_probs(l, off, h, t):
                n, kts = item(off, h, t), key_tiles(off, t)
                wait(pe, prob_ready, l, n)
                if n == 0:
                    wait(pe, v_ready, l, 0)
                if t >= 2 or h > 0:
                    wait(pe, probt_ready, l, n - 2)
                for b in range(len(kts)):
                    m = nc.tensor.transpose(psum[:, PT_BANK + n % 2, b * P:(b + 1) * P],
                                            prob[t][:, b * P:(b + 1) * P], ident[:])
                m.then_inc(probt_done.sem, 1)

            def weighted_values(l, off, pair):
                heads = (2 * pair, 2 * pair + 1)
                wait(pe, probt_ready, l, item(off, heads[1], TT - 1))
                if off or pair:
                    wait(pe, o_lo_ready, l, off // 2 + pair - 1)

                def product(h, kt, q, nq, first, last):
                    rows = head_rows(off, h)[0]
                    v = va[:, kt, rows] if off == 0 else vc[:, kt, h * HALF:(h + 1) * HALF]
                    return nc.tensor.matmul(psum[rows, O_BANK, q:q + nq], v, prob_t(h, [kt], q, nq),
                                            start=first, stop=last)
                if off == 0:
                    for t in range(TT):
                        kts = key_tiles(off, t)
                        for kt in kts:
                            for h in heads:
                                m = product(h, kt, t * P, P, kt == kts[0], kt == kts[-1])
                else:
                    for kt in range(TT):
                        for h in heads:
                            m = product(h, kt, kt * P, SEQ - kt * P, kt == 0, kt == TT - 1)
                m.then_inc(pv_done.sem, 1)

            def transpose_values(l, m, u):
                wait(pe, evac, l, u)
                bank = PT_BANK if m == 0 else SCORE_BANK + m % 2
                if m >= 3:
                    wait(pe, v_ready, l, m - 2)
                for t in range(TT):
                    r = nc.tensor.transpose(psum[:, bank, t * P:(t + 1) * P], tmp[u % 2][:, 2 + t * P:2 + (t + 1) * P],
                                            ident[:])
                r.then_inc(vt_done.sem, 1)

            def extra(l, u, gap):
                if (u, gap) == (1, 2):
                    sum_squares(l, 0)
                if (u, gap) == (2, 1):
                    spread_row_factors(l, 0)
                if (u, gap) == (U_C + 1, 0):
                    transpose_values(l, 0, U_C - 1)
                if U_C + 10 <= u < U_C + 14 and gap == 0:
                    transpose_values(l, u - (U_C + 10) + 1, u - 2)
                stages = head_at(u)
                if stages:
                    off, h_s, h_t, h_v = stages
                    if gap == 0 and h_v is not None and h_v % 2:
                        weighted_values(l, off, h_v // 2)
                    if h_t is not None:
                        transpose_probs(l, off, h_t, gap)
                    if h_s is not None:
                        scores(l, off, h_s, gap)

            with pe.Fori(0, DEPTH) as l:
                for u in range(U_OUT):
                    outs = unit_outs(u)
                    for o in outs:
                        pe.wait_ge(evac.sem, evac.after(l, o - (PROJ_BANKS if o >= PROJ_BANKS else PROJ_BANKS + 1)))
                    before = x_waits(l, 0) if u == 0 else None
                    if len(outs) == 1:
                        tiles = x_tiles(outs[0] % PROJ_BANKS)
                    else:
                        br, mp, _ = merge_group(u)
                        y_hi, y_lo = (ya_hi, ya_lo) if br == 1 else (ybc_hi, ybc_lo)
                        tiles = [(psum[:, o % PROJ_BANKS, :], y_hi[:, k, :], y_lo[:, k, :], k == 0, k == 3)
                                 for o in outs for k in range(4)]
                        if mp == 0:
                            if br == 0:
                                wait(pe, yb_hi_ready, l, 3)
                                wait(pe, convb, l, 19)
                            else:
                                wait(pe, o_hi_ready, l, 3 if br == 1 else 7)
                                wait(pe, o_lo_ready, l, 3 if br == 1 else 7)
                    weight_unit(l, u, u % 2, tiles, before, lambda gap, u=u: extra(l, u, gap))

                with pe.Fori(0, KT // 4) as i:
                    for j in range(4):
                        u = U_OUT + j
                        pe.wait_ge(evac.sem, evac.after(l, O_OUT + j - 3 + i * 4))
                        tiles = [(psum[:, j, :], mix_hi[:, k, :], mix_lo[:, k, :], k == 0, k == KT - 1)
                                 for k in range(KT)]

                        def mix_waits(k):
                            wait(pe, mix_hi_ready, l, k)
                            wait(pe, mix_lo_ready, l, k)
                        weight_unit(l, i * 4 + u, u % 2, tiles, mix_waits if j == 0 else None,
                                    late=2 if j == 0 else 0)

                def up_units(i, first=False):
                    for j in range(4):
                        u = U_UP + j

                        def norm_steps(gap, j=j):
                            if (j, gap) == (0, 3):
                                sum_squares(l, 1)
                            if (j, gap) == (1, 1):
                                spread_row_factors(l, 1)
                        pe.wait_ge(evac.sem, evac.after(l, O_UP + j - 4 + i * 4))
                        weight_unit(l, i * 4 + u, u % 2, x_tiles(j),
                                    x_waits(l, 1) if first and j == 0 else None, norm_steps if first else None)

                up_units(0, first=True)
                with pe.Fori(1, FF_T // 2) as i:
                    up_units(i)

                for u in range(U_DOWN, UNITS):
                    tiles = []
                    for i in range(TILES):
                        m, k = divmod((u - U_DOWN) * TILES + i, FF_T)
                        if k == 0 or i == 0:
                            wait(pe, evac, l, O_DOWN + m - 4)
                        tiles.append((psum[:, m % 4, :], ff_hi[:, k, :], ff_lo[:, k, :], k == 0, k == FF_T - 1))

                    def ff_waits(i, u=u):
                        pair = (u - U_DOWN) * TILES + i
                        if pair < FF_T:
                            wait(pe, ff_act, l, 4 * pair + 3)
                            wait(pe, ff_vec, l, 7 * pair + 6)
                    weight_unit(l, u, u % 2, tiles, ff_waits)
            sum_squares(DEPTH, 0)
            spread_row_factors(DEPTH, 0)

        @block.vector
        def _(dve):
            dve.sem_inc(evac.sem, evac.credit)
            nc.vector.memset(ones[:], 1.0)
            nc.vector.memset(minus_half[:], -0.5)
            for i in range(4):
                nc.vector.memset(tmp[i][:, 0:2], 0.0)
            for half, masked in ((0, (1, 0, 0, 1)), (1, (1, 1, 0, 0))):
                for chunk in range(4):
                    last = nc.vector.memset(mask_a[HALF * half:HALF * half + HALF, chunk * CHUNK:(chunk + 1) * CHUNK],
                                            MASKED if masked[chunk] else 0.0)
            last.then_inc(consts_set, 1)

            def unit_wait(l, u):
                dve.wait_ge(unit_steps.sem, unit_done(l, u))

            def scaled(dst, bank, factor=1.0):
                return nc.vector.scalar_tensor_tensor(dst, psum[:, bank, :], factor, rnorm[:], ALU.mult, ALU.mult)

            def add_square(l, norm, k, parity):
                wait(dve, sq_ready, l, norm * KT + k)
                nc.vector.tensor_tensor(sq_sum[:], sq_sum[:], tmp[parity][:, 2:], ALU.add).then_inc(sum_step.sem, 1)

            def lo_of_x(l, norm, k, gain):
                wait(dve, xhi_ready, l, norm * KT + k)
                nc.vector.scalar_tensor_tensor(xg_lo[:, k, :], x[:, k, :], gain, xg_hi[:, k, :].bitcast(F32),
                                               ALU.mult, ALU.subtract).then_inc(xlo_ready.sem, 1)

            def mean_square(l, norm):
                wait(dve, sumsq_done, l, norm)
                nc.vector.tensor_scalar(ms[:], psum[:, MS_BANK, 0:TT], 1.0 / D_MODEL, EPS, ALU.mult, ALU.add
                                        ).then_inc(ms_ready.sem, 1)

            def rope_out(l, u):
                dst = qa[:, u, :] if u < 4 else ka[:]
                wait(dve, evac, l, u)
                nc.vector.tensor_tensor(dst, wide[u % 2][:], rope_sb[:, 0, :], ALU.mult).then_inc(rope_mul.sem, 1)
                wait(dve, rot_done, l, u)
                nc.vector.tensor_tensor(wide[2 + u % 2][:], wide[2 + u % 2][:], rope_sb[:, 1, :], ALU.mult
                                        ).then_inc(rope_mul.sem, 1)
                wait(dve, rope_mul, l, 2 * u + 1)
                nc.vector.tensor_tensor(dst, dst, wide[2 + u % 2][:], ALU.add).then_inc(qk_ready.sem, 1)

            def yb_lo(l, c):
                wait(dve, yb_hi_ready, l, c)
                nc.vector.tensor_tensor(ybc_lo[:, c, :], wide[2 + c % 2][:], ybc_hi[:, c, :].bitcast(F32),
                                        ALU.subtract).then_inc(convb.sem, 1)

            def add_to_merged(l, mp, outs):
                for b, m in enumerate((2 * mp, 2 * mp + 1)):
                    wait(dve, evac, l, outs[b])
                    nc.vector.tensor_tensor(merged[:, m, :], merged[:, m, :], tmp[b][:, 2:], ALU.add
                                            ).then_inc(merged_sum.sem, 1)

            def mix_lo_part(l, m):
                wait(dve, mix_hi_ready, l, m)
                nc.vector.scalar_tensor_tensor(mix_lo[:, m, :], merged[:, m, :], 0.5, mix_hi[:, m, :].bitcast(F32),
                                               ALU.mult, ALU.subtract).then_inc(mix_lo_ready.sem, 1)

            def normalise(l, off, h, t):
                n, cols = item(off, h, t), seen(off, t)
                wait(dve, exp_done, l, n)
                if off == 0:
                    wait(dve, sink_done, l, n)
                    nc.vector.tensor_tensor(denom[:, n:n + 1], denom[:, n:n + 1], sink_e[:, n:n + 1], ALU.add
                                            ).then_inc(denom_done.sem, 1)
                    wait(dve, denom_done, l, n)
                nc.vector.reciprocal(denom[:, n:n + 1], denom[:, n:n + 1]).then_inc(recip_done.sem, 1)
                wait(dve, recip_done, l, n)
                nc.vector.tensor_scalar(prob[t][:, cols], prob[t][:, cols], denom[:, n:n + 1], None, ALU.mult
                                        ).then_inc(prob_ready.sem, 1)

            def split_qk_lo(l, slot):
                if not split_head(slot):
                    return
                off, h = split_head(slot)
                own, other, q, k = head_rows(off, h)
                wait(dve, qk_hi_ready, l, off + h)
                if off or h < 2:
                    nc.vector.tensor_tensor(k_lo[own, :], k, k_twice[own, h % 2, :].bitcast(F32), ALU.subtract)
                nc.vector.tensor_tensor(q_split[other, h % 2, :], q, q_split[own, h % 2, :].bitcast(F32), ALU.subtract
                                        ).then_inc(qk_lo_ready.sem, 1)

            def softmax_stage(l, slot):
                stages = head_at(slot)
                if not stages:
                    split_qk_lo(l, slot)
                    return
                off, h_s, h_t, h_v = stages
                if h_v is not None and h_v % 2:
                    hi, lo = (ya_hi, ya_lo) if off == 0 else (ybc_hi, ybc_lo)
                    wait(dve, o_hi_ready, l, (off + h_v) // 2)
                    nc.vector.tensor_tensor(lo[:, h_v // 2, :], psum[:, O_BANK, :],
                                            hi[:, h_v // 2, :].bitcast(F32), ALU.subtract).then_inc(o_lo_ready.sem, 1)
                if h_s is not None:
                    for t in range(TT):
                        n, cols = item(off, h_s, t), seen(off, t)
                        if off == 0:
                            head = h_s // 2 + 4 * (h_s % 2)
                            add = mask_a[:, 2 * P - (cols.stop - cols.start):]
                            start = neg_sink[:, head:head + 1]
                            if h_s == 0 and t == 0:
                                wait(dve, nsink_ready, l, 0)
                            if h_s == 0 and t:
                                nc.vector.memset(prob[t][:, 0:CHUNK], 0.0)
                        else:
                            add, start = bias[:, h_s, cols.stop - 1::-1], NO_MAX_YET
                        wait(dve, scores_done, l, n)
                        dve.sem_inc(scores_seen, 1)
                        nc.vector.tensor_tensor_reduce(
                            out=prob[t][:, cols], in0=psum[:, SCORE_BANK + n % 2, cols], in1=add,
                            scale=-1.0, scalar=start, op0=ALU.add, op1=ALU.min,
                            accum_out=neg_max[:, n:n + 1]).then_inc(logits_ready.sem, 1)
                        if t:
                            normalise(l, off, h_s, t - 1)
                        if t == 2:
                            split_qk_lo(l, slot)
                    normalise(l, off, h_s, TT - 1)

            def extend_bias_table():
                rows, near = DEPTH * C_HEADS, CHUNK
                far = REL_EXT - near - C_REL_SIZE
                dve.wait_ge(rel_in, 16)
                nc.vector.tensor_copy(rel_ext[0:rows, 0:near], rel_tab[0:rows, 0:1].to_broadcast([rows, near])
                                      ).then_inc(rel_built, 1)
                nc.vector.tensor_copy(rel_ext[0:rows, near:near + C_REL_SIZE], rel_tab[0:rows, :]).then_inc(rel_built, 1)
                nc.vector.tensor_copy(rel_ext[0:rows, near + C_REL_SIZE:REL_EXT],
                                      rel_tab[0:rows, C_REL_SIZE - 1:C_REL_SIZE].to_broadcast([rows, far])
                                      ).then_inc(rel_built, 1)

            dve.wait_ge(consts_set, 1)
            for k in range(KT):
                lo_of_x(0, 0, k, g0[:, k:k + 1])
                if k == 1:
                    extend_bias_table()
            for k in range(1, KT):
                if k > 1:
                    wait(dve, sum_step, 0, k - 2)
                add_square(0, 0, k, k % 2)
            dve.wait_ge(par_in, 16)

            with dve.Fori(0, DEPTH) as l:
                mean_square(l, 0)
                nc.vector.tensor_copy(par[:], par_all[:, bass.ds(l, 1), :].rearrange("p a n -> p (a n)")
                                      ).then_inc(par_ready.sem, 1)
                wait(dve, par_ready, l, 0)
                nc.vector.tensor_scalar(neg_sink[:], par[:, PSK:PSK + A_Q_HEADS], -1.0, None, ALU.mult
                                        ).then_inc(nsink_ready.sem, 1)
                for u in range(U_OUT):
                    outs = unit_outs(u)
                    banks = [o % PROJ_BANKS for o in outs]
                    unit_wait(l, u)
                    if u == 0:
                        wait(dve, rnorm_ready, l, 0)
                        dve.wait_ge(rel_stored, 16)
                        dve.wait_ge(rope_in, l * 16 + 16)
                    if u < 5:
                        scaled(wide[u % 2][:], banks[0], SCALE if u < 4 else 1.0).then_inc(evac.sem, 1)
                        if u:
                            rope_out(l, u - 1)
                    elif u == 5:
                        scaled(tmp[u % 2][:, 2:], banks[0]).then_inc(evac.sem, 1)
                        rope_out(l, 4)
                    elif u < U_C + 4:
                        scaled(qc[:, u - U_C, :], banks[0], SCALE).then_inc(evac.sem, 1)
                    elif u < U_C + 8:
                        scaled(kc[:, u - U_C - 4, :], banks[0]).then_inc(evac.sem, 1)
                    elif u < U_B:
                        scaled(tmp[u % 2][:, 2:], banks[0]).then_inc(evac.sem, 1)
                    elif u < U_MERGE:
                        c, part = divmod(u - U_B, 3)
                        y = wide[2 + c % 2]
                        scaled(wide[(0, 1, 4)[part]][:], banks[0]).then_inc(evac.sem, 1)
                        if part == 0 and c:
                            yb_lo(l, c - 1)
                        if part == 1:
                            wait(dve, evac, l, u)
                            nc.vector.tensor_tensor(tmp[c % 2][:, 2:], wide[0][:], wide[1][:], ALU.mult
                                                    ).then_inc(convb.sem, 1)
                        if part == 2:
                            wait(dve, tapb_done, l, c)
                            for tap in (1, 0):
                                nc.vector.scalar_tensor_tensor(
                                    y[:], tmp[c % 2][:, tap:tap + SEQ], par[:, PCB + 3 * c + tap:PCB + 3 * c + tap + 1],
                                    y[:], ALU.mult, ALU.add).then_inc(convb.sem, 1)
                                wait(dve, convb, l, 5 * c + 2 - tap)
                            wait(dve, evac, l, u)
                            nc.vector.tensor_tensor(y[:], y[:], wide[4][:], ALU.mult).then_inc(convb.sem, 1)
                    else:
                        br, mp, part = merge_group(u)
                        if part < 2:
                            if br == 2 or (br, mp > 0) == (1, True):
                                wait(dve, merged_sum, l, (br - 1) * KT + 2 * mp - 2 + part)
                            scaled(tmp[part][:, 2:], banks[0]).then_inc(evac.sem, 1)
                            if u == U_MERGE:
                                yb_lo(l, 3)
                            if br == 2 and part == 0 and mp:
                                mix_lo_part(l, 2 * mp - 2)
                                mix_lo_part(l, 2 * mp - 1)
                        else:
                            for b, m in enumerate((2 * mp, 2 * mp + 1)):
                                wait(dve, gate_ready, l, br * KT + m)
                                dst = merged[:, m, :] if br == 0 else tmp[b][:, 2:]
                                nc.vector.scalar_tensor_tensor(dst, tmp[2 + b][:, 2:], 1.0, psum[:, banks[b], :],
                                                               ALU.add, ALU.mult).then_inc(evac.sem, 1)
                            if br == 2:
                                add_to_merged(l, mp, outs)
                            if br == 2 and mp == 3:
                                mix_lo_part(l, 6)
                                mix_lo_part(l, 7)
                    if u == U_MERGE:
                        dve.wait_ge(bias_in, l * 16 + 16)
                        nc.vector.memset(bias[0:HALF, :, 0:CHUNK], MASKED).then_inc(bias_masked, 1)
                        dve.wait_ge(bias_masked, l + 1)
                    softmax_stage(l, u + 1)
                    if u >= U_MERGE and merge_group(u)[::2] == (1, 2):
                        add_to_merged(l, merge_group(u)[1], outs)

                def residual(bank, k):
                    nc.vector.tensor_tensor(x[:, k, :], x[:, k, :], psum[:, bank, :], ALU.add).then_inc(evac.sem, 1)

                for k in range(KT):
                    unit_wait(l, U_OUT + k)
                    residual(k % 4, k)
                    lo_of_x(l, 1, k, par[:, PG2 + k:PG2 + k + 1])
                    if k > 1:
                        wait(dve, sum_step, l, KT - 1 + k - 2)
                    if k:
                        add_square(l, 1, k, k % 2)
                mean_square(l, 1)

                def up_pair(i, b, first=False):
                    g_in_, v_in_, yg, yv, th = tmp[2 * b], tmp[2 * b + 1], wide[2 * b], wide[2 * b + 1], wide[4 + b]
                    for j in range(2):
                        unit_wait(l, i * 4 + (U_UP + 2 * b + j))
                        if first and j == 0:
                            wait(dve, rnorm_ready, l, 1)
                        scaled(tmp[2 * b + j][:, 2:], 2 * b + j).then_inc(evac.sem, 1)
                    for tap in (1, 0):
                        for j, (src, y) in enumerate(((g_in_, yg), (v_in_, yv))):
                            if tap == 1:
                                wait(dve, ff_act, l, 4 * b + j + i * 8)
                                wait(dve, evac, l, O_UP + 2 * b + j + i * 4)
                            else:
                                wait(dve, ff_vec, l, 7 * b + j + i * 14)
                            nc.vector.scalar_tensor_tensor(
                                y[:], src[:, tap:tap + SEQ], par[:, bass.ds(i * 6 + (PCF + 3 * (FF_T * j + b) + tap), 1)],
                                y[:], ALU.mult, ALU.add).then_inc(ff_vec.sem, 1)
                    wait(dve, ff_act, l, 4 * b + 2 + i * 8)
                    wait(dve, ff_vec, l, 7 * b + 3 + i * 14)
                    nc.vector.scalar_tensor_tensor(th[:], th[:], 1.0, yg[:], ALU.add, ALU.mult).then_inc(ff_vec.sem, 1)
                    wait(dve, ff_vec, l, 7 * b + 4 + i * 14)
                    nc.vector.scalar_tensor_tensor(th[:], th[:], 0.5, yv[:], ALU.mult, ALU.mult
                                                   ).then_inc(ff_vec.sem, 1)
                    wait(dve, ff_act, l, 4 * b + 3 + i * 8)
                    at = bass.ds(i * 2 + b, 1)
                    nc.vector.tensor_tensor(ff_lo[:, at, :].rearrange("p a t -> p (a t)"), th[:],
                                            ff_hi[:, at, :].rearrange("p a t -> p (a t)").bitcast(F32),
                                            ALU.subtract).then_inc(ff_vec.sem, 1)

                up_pair(0, 0, first=True)
                up_pair(0, 1)
                with dve.Fori(1, FF_T // 2) as i:
                    up_pair(i, 0)
                    up_pair(i, 1)

                for k in range(KT):
                    unit_wait(l, U_DOWN + (k * FF_T + FF_T - 1) // TILES)
                    residual(k % 4, k)

                    def add():
                        if k > 1:
                            wait(dve, sum_step, l + 1, k - 2)
                        if k:
                            add_square(l + 1, 0, k, k % 2)
                    if k == KT - 1:
                        add()
                    lo_of_x(l + 1, 0, k, par[:, PGN + k:PGN + k + 1])
                    if k < KT - 1:
                        add()
            mean_square(DEPTH, 0)
            wait(dve, rnorm_ready, DEPTH, 0)
            for k in range(POOL_OUT):
                nc.vector.scalar_tensor_tensor(x_out[:, k, :], x[:, k, :], par[:, PGN + k:PGN + k + 1], rnorm[:],
                                               ALU.mult, ALU.mult).then_inc(out_ready, 1)


def _units(w_in, w_o_a, w_o_b, w_o_c, w_out, w_up, w_down):
    heads = [h for j in range(PAIRS) for h in (j, j + A_Q_HEADS // A_KV_HEADS)]
    pair_rows = np.concatenate([np.arange(h * HEAD_DIM, (h + 1) * HEAD_DIM) for h in heads])
    stream = []
    for l in range(DEPTH):
        def tile(w, k, m):
            return w[k * P:(k + 1) * P, m * P:(m + 1) * P]

        def column(w, m):
            return [tile(w, k, m) for k in range(KT)]

        cols = np.arange(w_in.shape[2])
        at = np.cumsum([0, 512, 128, 128, 512, 512, 512, 512, 512, 512])
        cols[0:512] = pair_rows
        w = w_in[l][:, cols]
        q_a, k_a, v_a, b_b, c_b, u_b, q_c, k_c, v_c, gate = (int(c) // P for c in at)
        tiles = []
        for m in list(range(q_a, q_a + 4)) + [k_a, v_a] + list(range(q_c, q_c + 12)):
            tiles += column(w, m)
        for c in range(4):
            for m in (u_b + c, c_b + c, b_b + c):
                tiles += column(w, m)
        for branch, w_o in ((1, w_o_b[l]), (0, w_o_a[l][pair_rows]), (2, w_o_c[l])):
            for m in range(0, KT, 2):
                tiles += column(w, gate + branch * KT + m) + column(w, gate + branch * KT + m + 1)
                tiles += [tile(w_o, k, n) for n in (m, m + 1) for k in range(4)]
        for m in range(KT):
            tiles += column(w_out[l], m)
        for m in range(FF_T):
            tiles += column(w_up[l], m) + column(w_up[l], FF_T + m)
        tiles += [tile(w_down[l], k, m) for m in range(KT) for k in range(FF_T)]
        stream += tiles
    a = np.stack(stream).reshape(DEPTH * UNITS, TILES, P, P)
    return np.ascontiguousarray(a.transpose(0, 2, 1, 3)).reshape(DEPTH * UNITS, P, TILES * P)


def _by_feature(v):
    return np.moveaxis(v.reshape(v.shape[:-1] + (-1, P)), -1, 0)


def _rope_tables():
    half = HEAD_DIM // 2
    inv = np.float32(ROPE_THETA) ** (-np.arange(half, dtype=np.float32) / np.float32(half))
    angle = (np.arange(SEQ, dtype=np.float32)[None, :] * inv[:, None]).astype(np.float32)
    cos, sin = np.cos(angle), np.sin(angle)
    return np.stack([np.tile(cos, (4, 1)), np.concatenate([-sin, sin, -sin, sin])], axis=1).astype(np.float32)


def kernel(**inputs):
    import concourse.bacc as bacc
    from concourse.bass_utils import run_bass_kernel_spmd

    a = {name: np.asarray(v) for name, v in inputs.items()}
    g1 = [_by_feature(a["mix_norm_g"][l]) for l in range(DEPTH)] + [_by_feature(a["final_norm_g"])]
    params = []
    for l in range(DEPTH):
        conv_b = _by_feature(a["conv_b_w"][l])
        conv_f = _by_feature(a["ffn_conv_w"][l])
        params.append(np.concatenate([
            _by_feature(a["ffn_norm_g"][l]), g1[l + 1],
            conv_b.transpose(0, 2, 1).reshape(P, -1), conv_f.transpose(0, 2, 1).reshape(P, -1),
            np.broadcast_to(a["attn_sinks"][l], (P, A_Q_HEADS))], axis=1))
    arrays = {
        "xT": np.ascontiguousarray(a["x"][0].T),
        "weights": _units(*(a[n] for n in ("w_in", "w_o_a", "w_o_b", "w_o_c", "w_out", "w_up", "w_down"))),
        "g_first": np.ascontiguousarray(g1[0]),
        "params": np.ascontiguousarray(np.stack(params)),
        "rope": _rope_tables(),
        "rel": np.ascontiguousarray(a["rel_bias"].reshape(DEPTH * C_HEADS, C_REL_SIZE)),
    }
    nc = bacc.Bacc("TRN2", target_bir_lowering=False, num_devices=1)
    drams = [nc.dram_tensor(name, v.shape, mybir.dt.from_np(v.dtype), kind="ExternalInput").ap()
             for name, v in arrays.items()]
    out = nc.dram_tensor("outT", (D_MODEL, SEQ), F32, kind="ExternalOutput").ap()
    build_trunk(nc, *drams, out)
    r = run_bass_kernel_spmd(nc, [arrays], core_ids=[0])
    return np.ascontiguousarray(r.results[0]["outT"].T)[None]
```
